# Optimizing a Trainium2 kernel written in Bass

```python
import jax, jax.numpy as jnp
from jax import lax
import numpy as np

D_MODEL = 2048
BATCH = 1
SEQ = 256
DEPTH = 1

N_META = 16
D_MIX = D_MODEL
D_SC = D_MIX // 2
D_CF = D_MIX - D_SC
SC_WIDTH = 3
CF_WIDTH = 31
D_IN = 3 * D_SC + 2 * D_CF
D_FF = 5632
FFN_RES_SCALE = 0.5
EPS = 1e-6

kernel_name = "hymba_parallel_shortconv_conformer_macaron"

def rmsnorm(x, g):
    xf = x.astype(jnp.float32)
    y = xf * lax.rsqrt(jnp.mean(xf * xf, axis=-1, keepdims=True) + EPS)
    return (y * g.astype(jnp.float32)).astype(x.dtype)

def layernorm(x, g, b):
    xf = x.astype(jnp.float32)
    mu = jnp.mean(xf, axis=-1, keepdims=True)
    var = jnp.mean(jnp.square(xf - mu), axis=-1, keepdims=True)
    y = (xf - mu) * lax.rsqrt(var + EPS)
    return (y * g.astype(jnp.float32) + b.astype(jnp.float32)).astype(x.dtype)

def causal_dwconv(x, w):
    k, c = w.shape
    return lax.conv_general_dilated(
        x, w.astype(x.dtype)[:, None, :], window_strides=(1,), padding=[(k - 1, 0)],
        dimension_numbers=("NWC", "WIO", "NWC"), feature_group_count=c)

def swiglu(h, w_gate, w_up, w_down):
    return (jax.nn.silu(h @ w_gate) * (h @ w_up)) @ w_down

def setup_inputs(seed: int = 0) -> dict:
    key = jax.random.key(seed)
    ks = jax.random.split(key, 24)
    f32 = jnp.float32
    nrm = lambda k, shape, scale: (jax.random.normal(k, shape, f32) * scale).astype(f32)
    gain = lambda k, shape: 1.0 + 0.05 * jax.random.normal(k, shape, f32)
    L = DEPTH
    return {
        "x": jax.random.normal(ks[0], (BATCH, SEQ, D_MODEL), f32),
        "meta_tokens": nrm(ks[1], (N_META, D_MODEL), 1.0),
        "ffn1_norm": gain(ks[2], (L, D_MODEL)),
        "ffn1_w_gate": nrm(ks[3], (L, D_MODEL, D_FF), D_MODEL ** -0.5),
        "ffn1_w_up": nrm(ks[4], (L, D_MODEL, D_FF), D_MODEL ** -0.5),
        "ffn1_w_down": nrm(ks[5], (L, D_FF, D_MODEL), D_FF ** -0.5),
        "mix_norm": gain(ks[6], (L, D_MODEL)),
        "w_in": nrm(ks[7], (L, D_MODEL, D_IN), D_MODEL ** -0.5),
        "b_in": nrm(ks[8], (L, D_IN), 0.02),
        "conv_sc_w": nrm(ks[9], (L, SC_WIDTH, D_SC), SC_WIDTH ** -0.5),
        "conv_cf_w": nrm(ks[10], (L, CF_WIDTH, D_CF), CF_WIDTH ** -0.5),
        "conv_cf_b": nrm(ks[11], (L, D_CF), 0.02),
        "ln_cf_g": gain(ks[12], (L, D_CF)),
        "ln_cf_b": nrm(ks[13], (L, D_CF), 0.02),
        "w_out": nrm(ks[14], (L, D_MIX, D_MODEL), D_MIX ** -0.5),
        "ffn2_norm": gain(ks[15], (L, D_MODEL)),
        "ffn2_w_gate": nrm(ks[16], (L, D_MODEL, D_FF), D_MODEL ** -0.5),
        "ffn2_w_up": nrm(ks[17], (L, D_MODEL, D_FF), D_MODEL ** -0.5),
        "ffn2_w_down": nrm(ks[18], (L, D_FF, D_MODEL), D_FF ** -0.5),
        "final_norm": gain(ks[19], (D_MODEL,)),
    }

def token_mixing(h, w_in, b_in, conv_sc_w, conv_cf_w, conv_cf_b, ln_cf_g, ln_cf_b, w_out):
    u = h @ w_in + b_in.astype(h.dtype)
    b_sc = u[..., :D_SC]
    c_sc = u[..., D_SC:2 * D_SC]
    v_sc = u[..., 2 * D_SC:3 * D_SC]
    a_cf = u[..., 3 * D_SC:3 * D_SC + D_CF]
    g_cf = u[..., 3 * D_SC + D_CF:]
    y_sc = b_sc * causal_dwconv(c_sc * v_sc, conv_sc_w)
    z = a_cf * jax.nn.sigmoid(g_cf)
    z = causal_dwconv(z, conv_cf_w) + conv_cf_b.astype(z.dtype)
    y_cf = jax.nn.silu(layernorm(z, ln_cf_g, ln_cf_b))
    return jnp.concatenate([y_sc, y_cf], axis=-1) @ w_out

def reference(x, meta_tokens, ffn1_norm, ffn1_w_gate, ffn1_w_up, ffn1_w_down, mix_norm, w_in, b_in,
              conv_sc_w, conv_cf_w, conv_cf_b, ln_cf_g, ln_cf_b, w_out,
              ffn2_norm, ffn2_w_gate, ffn2_w_up, ffn2_w_down, final_norm):
    bsz = x.shape[0]
    meta = jnp.broadcast_to(meta_tokens.astype(x.dtype)[None], (bsz, N_META, x.shape[-1]))
    hs = jnp.concatenate([meta, x], axis=1)
    for l in range(DEPTH):
        hs = hs + FFN_RES_SCALE * swiglu(rmsnorm(hs, ffn1_norm[l]), ffn1_w_gate[l], ffn1_w_up[l], ffn1_w_down[l])
        hs = hs + token_mixing(rmsnorm(hs, mix_norm[l]), w_in[l], b_in[l], conv_sc_w[l], conv_cf_w[l],
                               conv_cf_b[l], ln_cf_g[l], ln_cf_b[l], w_out[l])
        hs = hs + FFN_RES_SCALE * swiglu(rmsnorm(hs, ffn2_norm[l]), ffn2_w_gate[l], ffn2_w_up[l], ffn2_w_down[l])
    out = rmsnorm(hs, final_norm)
    return out[:, N_META:]


_drawn_inputs = setup_inputs


def setup_inputs(seed=0):
    import zlib

    import numpy as np

    out = dict(_drawn_inputs(seed))
    spreads = {}
    factors = {'b_in': 2.828, 'conv_cf_b': 4.561, 'ln_cf_g': 2.959, 'ln_cf_b': 8.0, 'ffn2_norm': 3.503}
    for name, (base, spread) in spreads.items():
        noise = np.random.default_rng([zlib.crc32(name.encode()), seed]).standard_normal(out[name].shape)
        drawn = base * np.exp(spread * noise) if base else spread * noise
        out[name] = __import__('jax').numpy.asarray(drawn.astype(out[name].dtype))
    for name, factor in factors.items():
        out[name] = (out[name] * factor).astype(out[name].dtype)
    return out
```

```python
from contextlib import ExitStack

import concourse.bass as bass
from concourse import mybir

ALU = mybir.AluOpType
ACT = mybir.ActivationFunctionType
F32 = mybir.dt.float32
F32R = mybir.dt.float32r

P = 128
EPS = 1e-6
BLOCK = 1024
RING = 4
BANK = 512
SET = 4


def build(nc, x, meta_tokens, ffn1_norm, ffn1_w_gate, ffn1_w_up, ffn1_w_down, mix_norm, w_in, b_in,
          conv_sc_w, conv_cf_w, conv_cf_b, ln_cf_g, ln_cf_b, w_out,
          ffn2_norm, ffn2_w_gate, ffn2_w_up, ffn2_w_down, final_norm, out):
    D = x.shape[2]
    SEQ = x.shape[1]
    META = meta_tokens.shape[0]
    T = META + SEQ
    FF = ffn1_w_gate.shape[2]
    KD = D // P
    KF = FF // P
    DS = conv_sc_w.shape[2]
    KS = DS // P
    SCW = conv_sc_w.shape[1]
    CFW = conv_cf_w.shape[1]
    PAD = CFW - 1 - META
    HALVES = SEQ // P
    ALL = slice(0, T)
    KEPT = slice(META, T)

    G_FF = KF // 2
    G_D = KD // SET
    G_MIX = KS // 2
    G_B = KS // SET
    N_GU = 2 * KD // 4
    N_DOWN = KF // 2
    N_B = KD // 2
    N_OUT = KS // 2

    sizes = [("gu1", G_FF, N_GU), ("down1", G_D, N_DOWN), ("ag", G_MIX, N_GU), ("cv", G_MIX, N_GU),
             ("b", G_B, N_B), ("out_sc", G_D, N_OUT), ("out_cf", G_D, N_OUT),
             ("gu2", G_FF, N_GU), ("down2", G_D, N_DOWN)]
    block0, group0, n_groups, n_blocks = {}, {}, {}, {}
    blocks = groups = 0
    for name, n_g, n_b in sizes:
        block0[name], group0[name], n_groups[name], n_blocks[name] = blocks, groups, n_g, n_b
        blocks += n_g * n_b
        groups += n_g
        assert n_g % 2 == 0 and blocks % RING == 0
    before = {b[0]: a[0] for a, b in zip(sizes, sizes[1:])}

    with ExitStack() as ctx:
        def sb(name, shape, dt=F32):
            return ctx.enter_context(nc.sbuf_tensor(name, shape, dt))

        def sem(name):
            return ctx.enter_context(nc.semaphore(name))

        ps = ctx.enter_context(nc.psum_tensor("ps", [P, 2 * SET, BANK], F32))

        sb("x_region", [P, 2 * KD * T])
        x_at = nc.sbuf_base - 4 * 2 * KD * T
        sb("a_region", [P, 2 * KF * T])
        a_at = nc.sbuf_base - 4 * 2 * KF * T

        raw = [sb(f"raw{i}", [P, BLOCK]) for i in range(RING)]
        w_hi = [sb(f"w_hi{i}", [P, BLOCK], F32R) for i in range(RING)]
        w_lo = [sb(f"w_lo{i}", [P, BLOCK], F32R) for i in range(RING)]
        res = sb("res", [P, KD, T])
        t1 = sb("t1", [P, 2, T])
        t2 = sb("t2", [P, 2, T])
        rstd = sb("rstd", [P, T])
        sq_sum = sb("sq_sum", [P, T])
        sq = sb("sq", [P, 2, T])
        step = sb("step", [P, 3, T])
        par = sb("par", [P, 4, P])
        ident = sb("ident", [P, P])
        ones = sb("ones", [P, P])
        tok = sb("tok", [P, 4, HALVES])

        def at(name, offset, shape, dt=F32):
            return nc.alloc_sbuf_tensor_at(name, shape, dt, offset=offset)

        x_hi = at("x_hi", x_at, [P, KD, T], F32R)
        x_lo = at("x_lo", x_at + 4 * KD * T, [P, KD, T], F32R)
        o_tile = at("o_tile", x_at, [P, SET, SEQ])
        o_tok = at("o_tok", x_at + 4 * SET * SEQ, [P, HALVES, D])
        a_hi = at("a_hi", a_at, [P, KF, T], F32R)
        a_lo = at("a_lo", a_at + 4 * KF * T, [P, KF, T], F32R)
        x_tok = at("x_tok", a_at, [P, HALVES, D])
        m_tok = at("m_tok", a_at + 4 * HALVES * D, [P, D])
        par_rows = at("par_rows", a_at + 4 * (HALVES + 1) * D, [P, 4, P])
        tile_bytes = 4 * SEQ
        y_hi = at("y_hi", a_at, [P, 2 * KS, SEQ], F32R)
        y_lo = at("y_lo", a_at + 2 * KS * tile_bytes, [P, 2 * KS, SEQ], F32R)
        y_f = at("y_f", a_at + 4 * KS * tile_bytes, [P, KS, SEQ])
        cs = at("cs", a_at + 5 * KS * tile_bytes, [P, KS, SEQ])
        zc = at("zc", a_at + 6 * KS * tile_bytes, [P, KS, SEQ])
        z = at("z", a_at + 7 * KS * tile_bytes, [P, KS, PAD + T])
        ln_at = a_at + 7 * KS * tile_bytes + 4 * KS * (PAD + T)
        ln_sum = at("ln_sum", ln_at, [P, SEQ])
        ln_mu = at("ln_mu", ln_at + tile_bytes, [P, SEQ])
        ln_rstd = at("ln_rstd", ln_at + 2 * tile_bytes, [P, SEQ])
        assert ln_at + 3 * tile_bytes <= a_at + 4 * 2 * KF * T

        rows0 = [("ffn1", ffn1_norm[0], KD), ("mix", mix_norm[0], KD), ("ffn2", ffn2_norm[0], KD),
                 ("final", final_norm, KD), ("cf_b", conv_cf_b[0], KS), ("ln_g", ln_cf_g[0], KS),
                 ("ln_b", ln_cf_b[0], KS)]
        row0, used = {}, 0
        for name, _, n in rows0:
            row0[name] = used
            used += n
        row0["sc_w"] = used
        n_rows = [used + SCW * KS, b_in.shape[1] // P, P, CFW * KS - P]

        def param(name, i):
            return par[:, 0, row0[name] + i:row0[name] + i + 1]

        def bias_in(i):
            return par[:, 1, i:i + 1]

        def cf_tap(k, c):
            row = k * KS + c
            return par[:, 2 + row // P, row % P:row % P + 1]

        raw_loaded = [sem(f"raw_loaded{i}") for i in range(RING)]
        hi_ready = sem("hi_ready")
        lo_ready = sem("lo_ready")
        block_used = sem("block_used")
        emptied = sem("emptied")
        par_loaded, x_loaded = sem("par_loaded"), [sem(f"x_loaded{i}") for i in range(5)]
        ones_set, ident_zero, ident_set = sem("ones_set"), sem("ident_zero"), sem("ident_set")
        par_turned, par_ready, x_turned = sem("par_turned"), sem("par_ready"), sem("x_turned")
        gain_of = {"start": "ffn1", "down1": "mix", "out_cf": "ffn2", "down2": "final"}
        xhi_ready, xlo_ready, sq_ready, sum_ready, stats_done, var_ready, sd_ready, newton = (
            {n: sem(f"{what}_{n}") for n in gain_of}
            for what in ("xhi_ready", "xlo_ready", "sq_ready", "sum_ready", "stats_done", "var_ready",
                         "sd_ready", "newton"))
        silu_ready, prod_ready, ahi_ready, alo_ready = (
            {n: sem(f"{what}_{n}") for n in ("gu1", "gu2")}
            for what in ("silu_ready", "prod_ready", "ahi_ready", "alo_ready"))
        pad_set, sig_ready, z_ready = sem("pad_set"), sem("sig_ready"), sem("z_ready")
        c_ready, cv_ready, sc_step = sem("c_ready"), sem("cv_ready"), sem("sc_step")
        cf_step, ln_added = sem("cf_step"), sem("ln_added")
        ysc_ready, ysc_hi, ysc_lo = sem("ysc_ready"), sem("ysc_hi"), sem("ysc_lo")
        ln_mean_done, ln_mu_set, centred = sem("ln_mean_done"), sem("ln_mu_set"), sem("centred")
        ln_sq, ln_var_sum, ln_var_done = sem("ln_sq"), sem("ln_var_sum"), sem("ln_var_done")
        ln_var, ln_sd, ln_newton, normed = sem("ln_var"), sem("ln_sd"), sem("ln_newton"), sem("normed")
        ycf_ready, ycf_hi, ycf_lo = sem("ycf_ready"), sem("ycf_hi"), sem("ycf_lo")
        o_turned, o_copied_s, o_copied_v = sem("o_turned"), sem("o_copied_s"), sem("o_copied_v")
        o_scaled_s, o_scaled_v, stored = sem("o_scaled_s"), sem("o_scaled_v"), sem("stored")

        def before_block(phase, g, i):
            return block0[phase] + i + n_blocks[phase] * g

        def slot(phase, g, i):
            return (n_blocks[phase] * g + i) % RING if isinstance(g, int) else i % RING

        def turn(phase, g, i):
            if isinstance(g, int):
                return (block0[phase] + n_blocks[phase] * g + i) // RING
            return (block0[phase] + i) // RING + n_blocks[phase] // RING * g

        def banks_before(phase, g):
            return KD + SET * group0[phase] + SET * g

        def previous(phase, g):
            if not isinstance(g, int) or g > 0:
                return phase, g - 1
            return (before[phase], n_groups[before[phase]] - 1) if phase in before else ("", 0)

        def over_groups(engine, phase, body):
            n = n_groups[phase]
            body(0, 0)
            if n > SET:
                with engine.Fori(1, n - 1, 2) as g:
                    body(g, 1)
                    body(g + 1, 0)
            else:
                for g in range(1, n - 1):
                    body(g, g % 2)
            if n > 1:
                body(n - 1, 1)

        width = {"gu1": T, "down1": T, "ag": T, "cv": T, "b": SEQ, "out_sc": SEQ, "out_cf": SEQ,
                 "gu2": SEQ, "down2": SEQ}

        def tokens(phase):
            return slice(0, T) if width[phase] == T else slice(META, T)

        block = ctx.enter_context(nc.Block())

        @block.sync
        def _(sp):
            for i in range(4):
                cols = slice(i * (D // 4), (i + 1) * (D // 4))
                sp.dma_start(x_tok[:, :, cols],
                             x[0, :, cols].rearrange("(h p) d -> p h d", p=P)).then_inc(x_loaded[i], 16)

            def load(phase, g, i, src, n):
                ahead, s = before_block(phase, g, i), slot(phase, g, i)
                if not isinstance(ahead, int) or ahead >= RING:
                    sp.wait_ge(lo_ready, ahead - (RING - 1))
                sp.dma_start(raw[s][:, :].rearrange("p (c n) -> p c n", n=n), src).then_inc(raw_loaded[s], 16)

            def paired(phase, wa, wb, col_a, col_b):
                rows = [w.rearrange("(q c p) n -> q p c n", c=4, p=P) for w in (wa, wb)]

                def body(g, parity):
                    for i in range(n_blocks[phase]):
                        src = rows[i % 2][i // 2, :, :, bass.ds(g * 256 + (col_a, col_b)[i % 2], 256)]
                        load(phase, g, i, src, 256)
                over_groups(sp, phase, body)

            def single(phase, w, first_row):
                rows = w.rearrange("(k c p) n -> k p c n", c=2, p=P)

                def body(g, parity):
                    for i in range(n_blocks[phase]):
                        load(phase, g, i, rows[first_row // (2 * P) + i, :, :, bass.ds(g * 512, 512)], 512)
                over_groups(sp, phase, body)

            paired("gu1", ffn1_w_gate[0], ffn1_w_up[0], 0, 0)
            single("down1", ffn1_w_down[0], 0)
            paired("ag", w_in[0], w_in[0], 3 * DS, 4 * DS)
            paired("cv", w_in[0], w_in[0], DS, 2 * DS)
            single("b", w_in[0], 0)
            single("out_sc", w_out[0], 0)
            single("out_cf", w_out[0], DS)
            paired("gu2", ffn2_w_gate[0], ffn2_w_up[0], 0, 0)
            single("down2", ffn2_w_down[0], 0)

            last = (KD - SET) * P
            for i, cols in enumerate((slice(0, last), slice(last, D))):
                sp.wait_ge(o_scaled_s, i + 1)
                sp.dma_start(out[0, 0:P, cols], o_tok[:, 0, cols]).then_inc(stored, 16)
                sp.wait_ge(o_scaled_v, i + 1)
                sp.dma_start(out[0, P:2 * P, cols], o_tok[:, 1, cols]).then_inc(stored, 16)
            sp.wait_ge(stored, 64)

        @block.gpsimd
        def _(pool):
            pool.memset(ident[:, :], 0.0).then_inc(ident_zero, 1)
            pool.wait_ge(ident_zero, 1)
            pool.affine_select(out=ident[:, :], in_=ident[:, :], compare_op=ALU.not_equal, fill=1.0, base=0,
                               pattern=[[-1, P]], channel_multiplier=1).then_inc(ident_set, 1)

        @block.tensor
        def _(pe):
            pe.wait_ge(ident_set, 1)
            pe.wait_ge(par_loaded, 16 * (len(rows0) + 4))
            for s in range(4):
                pe.transpose(ps[:, 7, s * P:s * P + n_rows[s]], par_rows[0:n_rows[s], s, :],
                             ident[0:n_rows[s], 0:n_rows[s]]).then_inc(par_turned, 1)
            pe.wait_ge(x_loaded[4], 16)
            for c in range(KD):
                if c % (KD // 4) == 0:
                    pe.wait_ge(x_loaded[c // (KD // 4)], 16)
                if c == 7:
                    pe.wait_ge(par_ready, 4)
                if c >= 8:
                    pe.wait_ge(emptied, c - 7)
                cols = slice(c * P, (c + 1) * P)
                pe.transpose(ps[:, c % 8, 0:META], m_tok[0:META, cols], ident[0:META, 0:META])
                for h in range(HALVES):
                    m = pe.transpose(ps[:, c % 8, META + h * P:META + (h + 1) * P], x_tok[:, h, cols], ident[:, :])
                m.then_inc(x_turned, 1)

            def product(bank, n, w_high, w_low, act_high, act_low, first, last):
                dst = ps[:, bank, 0:n]
                pe.matmul(dst, w_high, act_high, start=first, stop=False)
                pe.matmul(dst, w_high, act_low, start=False, stop=False)
                return pe.matmul(dst, w_low, act_high, start=False, stop=last)

            def start_group(phase, g):
                pe.wait_ge(emptied, banks_before(phase, g) - SET)

            def start_block(phase, g, i):
                pe.wait_ge(lo_ready, before_block(phase, g, i) + 1)

            def square_sums(norm, phase):
                pe.wait_ge(sum_ready[norm], KD)
                pe.matmul(ps[:, 7, 0:width[phase]], ones[:, :], sq_sum[:, tokens(phase)],
                          start=True, stop=True).then_inc(stats_done[norm], 1)

            def paired(phase, norm):
                toks = tokens(phase)

                def body(g, parity):
                    first_group = isinstance(g, int) and g == 0
                    start_group(phase, g)
                    if norm and isinstance(g, int) and g == 1:
                        pe.wait_ge(var_ready[norm], 1)
                    for i in range(n_blocks[phase]):
                        s = slot(phase, g, i)
                        start_block(phase, g, i)
                        for j in range(2):
                            for c in range(4):
                                k = 4 * (i // 2) + c
                                if norm and first_group and i % 2 == 0 and j == 0:
                                    pe.wait_ge(xlo_ready[norm], k + 1)
                                cols = slice(c * 256 + j * P, c * 256 + (j + 1) * P)
                                m = product(SET * parity + 2 * (i % 2) + j, width[phase],
                                            w_hi[s][:, cols], w_lo[s][:, cols],
                                            x_hi[:, k, toks], x_lo[:, k, toks], k == 0, k == KD - 1)
                        m.then_inc(block_used, 1)
                        if norm and first_group and i == 3:
                            square_sums(norm, phase)
                over_groups(pe, phase, body)

            def single_group(phase, g, parity, high, low, first_k, toks, n_k, ready, per_block, extra=None):
                start_group(phase, g)
                for i in range(n_blocks[phase]):
                    s = slot(phase, g, i) if isinstance(g, int) else (n_blocks[phase] * parity + i) % RING
                    start_block(phase, g, i)
                    if ready is not None and isinstance(g, int) and g == 0:
                        pe.wait_ge(ready, per_block(i))
                    for j in range(SET):
                        for c in range(2):
                            k = 2 * i + c
                            cols = slice(c * 512 + j * P, c * 512 + (j + 1) * P)
                            m = product(SET * parity + j, width[phase], w_hi[s][:, cols], w_lo[s][:, cols],
                                        high[:, first_k + k, toks], low[:, first_k + k, toks],
                                        k == 0, k == n_k - 1)
                    m.then_inc(block_used, 1)
                    if extra:
                        extra(n_blocks[phase] * g + i)

            def down(phase, gate_up, extra=None):
                for g in range(G_D):
                    single_group(phase, g, g % 2, a_hi, a_lo, 0, slice(0, width[phase]), KF,
                                 alo_ready[gate_up], lambda i: i + 1, extra)

            def layernorm_sums(b):
                if b == 1:
                    pe.wait_ge(ln_added, KS)
                    pe.wait_ge(emptied, banks_before("out_sc", 0))
                    pe.matmul(ps[:, SET, SEQ:2 * SEQ], ones[:, :], ln_sum[:, :],
                              start=True, stop=True).then_inc(ln_mean_done, 1)
                if b == 5:
                    pe.wait_ge(ln_var_sum, 1)
                    pe.matmul(ps[:, 0, SEQ:2 * SEQ], ones[:, :], ln_sum[:, :],
                              start=True, stop=True).then_inc(ln_var_done, 1)
                if b == SET - 1:
                    pe.wait_ge(ln_mu_set, 1)
                if b == 2 * SET - 1:
                    pe.wait_ge(ln_var, 1)

            def turn_output(g):
                pe.wait_ge(xhi_ready["down2"], SET * (g + 1))
                for j in range(SET):
                    for h in range(HALVES):
                        at_col = SEQ + (j % 2) * P
                        m = pe.transpose(ps[:, SET * (g % 2) + 2 * h + j // 2, at_col:at_col + P],
                                         o_tile[:, j, h * P:(h + 1) * P], ident[:, :])
                m.then_inc(o_turned, 1)

            def output_between(b):
                g, i = divmod(b, n_blocks["down2"])
                if g >= 1 and i == 6:
                    turn_output(g - 1)
                if g >= 1 and i == n_blocks["down2"] - 1:
                    pe.wait_ge(o_copied_s, g)
                    pe.wait_ge(o_copied_v, g)

            pe.wait_ge(ones_set, 1)
            paired("gu1", "start")
            down("down1", "gu1")
            paired("ag", "down1")
            paired("cv", None)
            for g in range(G_B):
                single_group("b", g, g % 2, x_hi, x_lo, 0, tokens("b"), KD, None, None)
            for g in range(G_D):
                single_group("out_sc", g, g % 2, y_hi, y_lo, 0, slice(0, SEQ), KS,
                             ysc_lo, lambda i: i // 2 + 1, layernorm_sums)
            for g in range(G_D):
                single_group("out_cf", g, g % 2, y_hi, y_lo, KS, slice(0, SEQ), KS,
                             ycf_lo, lambda i: i // 2 + 1)
            paired("gu2", "out_cf")
            down("down2", "gu2", output_between)
            turn_output(G_D - 1)
            pe.wait_ge(sum_ready["down2"], KD)
            for h in range(HALVES):
                m = pe.matmul(ps[:, 0, h:h + 1], sq_sum[:, META + h * P:META + (h + 1) * P], ones[:, 0:1],
                              start=True, stop=True)
            m.then_inc(stats_done["down2"], 1)

        @block.scalar
        def _(act):
            for name, src, n in rows0:
                act.dma_start(par_rows[row0[name]:row0[name] + n, 0, :],
                              src.rearrange("(r p) -> r p", p=P)).then_inc(par_loaded, 16)
            act.dma_start(par_rows[row0["sc_w"]:n_rows[0], 0, :],
                          conv_sc_w[0].rearrange("k (c p) -> (k c) p", p=P)).then_inc(par_loaded, 16)
            act.dma_start(par_rows[0:n_rows[1], 1, :],
                          b_in[0].rearrange("(r p) -> r p", p=P)).then_inc(par_loaded, 16)
            taps = conv_cf_w[0].rearrange("k (c p) -> (k c) p", p=P)
            act.dma_start(par_rows[0:P, 2, :], taps[0:P, :]).then_inc(par_loaded, 16)
            act.dma_start(par_rows[0:n_rows[3], 3, :], taps[P:P + n_rows[3], :]).then_inc(par_loaded, 16)
            act.dma_start(m_tok[0:META, :], meta_tokens).then_inc(x_loaded[4], 16)

            def high(phase, g, i):
                s = slot(phase, g, i)
                act.wait_ge(raw_loaded[s], 16 * turn(phase, g, i) + 16)
                ahead = before_block(phase, g, i)
                if not isinstance(ahead, int) or ahead >= RING:
                    act.wait_ge(block_used, ahead - (RING - 1))
                act.activation(w_hi[s][:, :], raw[s][:, :], ACT.Copy).then_inc(hi_ready, 1)

            def norm_operand(phase, norm, g, j):
                t, toks = SET * g + j, tokens(phase)
                act.wait_ge(emptied, t + 1 if norm == "start" else banks_before(norm, g) + j + 1)
                dst = x_hi[:, t, toks]
                if norm == "down2":
                    if g >= 1 and j == 0:
                        act.wait_ge(o_turned, g)
                    dst = o_tile[:, j, :]
                act.activation(dst, res[:, t, toks], ACT.Copy,
                               scale=param(gain_of[norm], t)).then_inc(xhi_ready[norm], 1)
                if t >= 2:
                    act.wait_ge(sum_ready[norm], t - 1)
                act.activation(sq[:, t % 2, toks], res[:, t, toks], ACT.Square).then_inc(sq_ready[norm], 1)

            def root(norm, phase):
                act.wait_ge(var_ready[norm], 1)
                act.activation(step[:, 1, tokens(phase)], step[:, 0, tokens(phase)],
                               ACT.Sqrt).then_inc(sd_ready[norm], 1)

            def finish(now, phase, g, at_step):
                read = banks_before(phase, g) if phase else 0
                if phase in ("gu1", "gu2"):
                    w = width[phase]
                    if at_step == 0:
                        act.wait_ge(emptied, read + 2)
                        act.activation(t1[:, :, 0:w], t1[:, :, 0:w], ACT.Silu).then_inc(silu_ready[phase], 1)
                    else:
                        act.wait_ge(prod_ready[phase], g + 1)
                        act.activation(a_hi[:, bass.ds(2 * g, 2), 0:w], t2[:, :, 0:w],
                                       ACT.Copy).then_inc(ahi_ready[phase], 1)
                if phase in ("down1", "down2"):
                    for j in (0, 1) if at_step == 0 else (2, 3):
                        norm_operand("ag" if phase == "down1" else "down2", phase, g, j)
                if phase == "out_cf" and at_step == 0:
                    for j in range(SET):
                        norm_operand("gu2", phase, g, j)
                if phase == "ag" and at_step == 0:
                    act.wait_ge(emptied, read + 4)
                    for j in range(2):
                        act.activation(t2[:, j, :], t2[:, j, :], ACT.Sigmoid,
                                       bias=bias_in(4 * KS + 2 * g + j)).then_inc(sig_ready, 1)
                if phase == "cv" and at_step == 0:
                    act.wait_ge(emptied, read + 2)
                    for j in range(2):
                        act.activation(t1[:, j, :], t1[:, j, :], ACT.Identity,
                                       bias=bias_in(KS + 2 * g + j)).then_inc(c_ready, 1)
                if phase == "b" and at_step == 0:
                    act.wait_ge(ysc_ready, SET * (g + 1))
                    act.activation(y_hi[:, SET * g:SET * (g + 1), :], y_f[:, SET * g:SET * (g + 1), :],
                                   ACT.Copy).then_inc(ysc_hi, 1)

            def layernorm(b):
                if b == 6:
                    act.wait_ge(centred, 1)
                    act.wait_ge(ysc_lo, G_B)
                    act.activation(y_f[:, :, :], zc[:, :, :], ACT.Square).then_inc(ln_sq, 1)
                if b == 9:
                    act.wait_ge(ln_var, 1)
                    act.activation(step[:, 1, 0:SEQ], step[:, 0, 0:SEQ], ACT.Sqrt).then_inc(ln_sd, 1)
                if b in (11, 12):
                    half = slice(SET * (b - 11), SET * (b - 10))
                    act.wait_ge(normed, 1)
                    for c in range(half.start, half.stop):
                        act.activation(y_f[:, c, :], zc[:, c, :], ACT.Silu, scale=param("ln_g", c),
                                       bias=param("ln_b", c)).then_inc(ycf_ready, 1)
                    act.wait_ge(ycf_ready, half.stop)
                    act.activation(y_hi[:, KS + half.start:KS + half.stop, :], y_f[:, half, :],
                                   ACT.Copy).then_inc(ycf_hi, 1)

            act.wait_ge(par_turned, 4)
            for s in range(4):
                m = act.activation(par[:, s, 0:n_rows[s]], ps[:, 7, s * P:s * P + n_rows[s]], ACT.Copy)
                m.then_inc(par_ready, 1)
            act.wait_ge(par_ready, 4)
            for c in range(KD):
                norm_operand("gu1", "start", c // SET, c % SET)
                if c % 2 and c // 2 in range(1, 1 + RING):
                    high("gu1", 0, c // 2 - 1)

            def phase_blocks(phase, norm=None, between=None):
                def body(g, parity):
                    for i in range(n_blocks[phase]):
                        if not (phase == "gu1" and isinstance(g, int) and g == 0 and i < RING):
                            high(phase, g, i)
                        if i in (3, 4):
                            finish(phase, *previous(phase, g), i - 3)
                        if norm and isinstance(g, int) and g == 0 and i == 7:
                            root(norm, phase)
                        if between:
                            between(n_blocks[phase] * g + i)
                over_groups(act, phase, body)

            def turned_output(b):
                g, i = divmod(b, n_blocks["down2"])
                if g >= 1 and i == 10:
                    act.wait_ge(o_turned, g)
                    bank = SET * ((g - 1) % 2)
                    act.activation(o_tok[:, 0, (g - 1) * 512:g * 512].rearrange("p (j n) -> p j n", n=2 * P),
                                   ps[:, bank:bank + 2, SEQ:2 * SEQ],
                                   ACT.Copy).then_inc(o_copied_s, 1)

            phase_blocks("gu1", "start")
            phase_blocks("down1")
            phase_blocks("ag", "down1")
            phase_blocks("cv")
            phase_blocks("b")
            phase_blocks("out_sc", None, layernorm)
            phase_blocks("out_cf")
            phase_blocks("gu2", "out_cf")
            phase_blocks("down2", None, turned_output)
            finish("", "down2", G_D - 1, 0)
            finish("", "down2", G_D - 1, 1)
            act.wait_ge(var_ready["down2"], 1)
            act.activation(tok[:, 1, :], tok[:, 0, :], ACT.Sqrt).then_inc(sd_ready["down2"], 1)
            act.wait_ge(newton["down2"], 5)
            last = (KD - SET) * P
            act.wait_ge(o_copied_s, G_D - 1)
            act.activation(o_tok[:, 0, 0:last], o_tok[:, 0, 0:last], ACT.Copy,
                           scale=tok[:, 3, 0:1]).then_inc(o_scaled_s, 1)
            act.wait_ge(o_turned, G_D)
            act.activation(o_tok[:, 0, last:D].rearrange("p (j n) -> p j n", n=2 * P),
                           ps[:, SET:SET + 2, SEQ:2 * SEQ], ACT.Copy,
                           scale=tok[:, 3, 0:1]).then_inc(o_scaled_s, 1)

        @block.vector
        def _(dve):
            dve.memset(ones[:, :], 1.0).then_inc(ones_set, 1)

            def low(phase, g, i):
                s = slot(phase, g, i)
                dve.wait_ge(hi_ready, before_block(phase, g, i) + 1)
                dve.tensor_tensor(w_lo[s][:, :], raw[s][:, :], w_hi[s][:, :].bitcast(F32),
                                  ALU.subtract).then_inc(lo_ready, 1)

            def norm_operand(phase, norm, g, j):
                t, toks = SET * g + j, tokens(phase)
                if norm != "down2":
                    dve.wait_ge(xhi_ready[norm], t + 1)
                    dve.scalar_tensor_tensor(x_lo[:, t, toks], res[:, t, toks], param(gain_of[norm], t),
                                             x_hi[:, t, toks].bitcast(F32), ALU.mult,
                                             ALU.subtract).then_inc(xlo_ready[norm], 1)
                dve.wait_ge(sq_ready[norm], t + 1)
                if t == 0:
                    dve.tensor_copy(sq_sum[:, toks], sq[:, 0, toks]).then_inc(sum_ready[norm], 1)
                else:
                    dve.wait_ge(sum_ready[norm], t)
                    dve.tensor_tensor(sq_sum[:, toks], sq_sum[:, toks], sq[:, t % 2, toks],
                                      ALU.add).then_inc(sum_ready[norm], 1)

            def inverse_root(dst, var, sd, y, q, sd_done, steps):
                dve.wait_ge(sd_done, 1)
                dve.reciprocal(y, sd).then_inc(steps, 1)
                dve.wait_ge(steps, 1)
                dve.tensor_tensor(q, var, y, ALU.mult).then_inc(steps, 1)
                dve.wait_ge(steps, 2)
                dve.tensor_tensor(q, q, y, ALU.mult).then_inc(steps, 1)
                dve.wait_ge(steps, 3)
                dve.tensor_scalar(q, q, -0.5, 1.5, ALU.mult, ALU.add).then_inc(steps, 1)
                dve.wait_ge(steps, 4)
                dve.tensor_tensor(dst, q, y, ALU.mult).then_inc(steps, 1)
                dve.wait_ge(steps, 5)

            def over_two(row, w, n=2):
                return row.unsqueeze(1).broadcast_to([P, n, w])

            def finish(phase, g, at_step):
                if not phase:
                    return
                bank = SET * ((g if isinstance(g, int) else parity_of[0]) % 2)
                w, toks = width[phase], tokens(phase)
                read = banks_before(phase, g)
                ended = before_block(phase, g, n_blocks[phase])
                if phase in ("gu1", "gu2", "ag", "cv"):
                    if at_step == 0:
                        factor = over_two(rstd[:, toks], w)
                        dve.wait_ge(block_used, ended)
                        dve.tensor_tensor(t1[:, :, 0:w], ps[:, bank:bank + 2, 0:w], factor,
                                          ALU.mult).then_inc(emptied, 2)
                        dve.tensor_tensor(t2[:, :, 0:w], ps[:, bank + 2:bank + 4, 0:w], factor,
                                          ALU.mult).then_inc(emptied, 2)
                if phase in ("gu1", "gu2"):
                    if at_step == 1:
                        dve.wait_ge(silu_ready[phase], g + 1)
                        dve.wait_ge(emptied, read + 4)
                        dve.tensor_tensor(t2[:, :, 0:w], t1[:, :, 0:w], t2[:, :, 0:w],
                                          ALU.mult).then_inc(prod_ready[phase], 1)
                    if at_step == 2:
                        dve.wait_ge(ahi_ready[phase], g + 1)
                        pair = bass.ds(2 * g, 2)
                        dve.tensor_tensor(a_lo[:, pair, 0:w], t2[:, :, 0:w], a_hi[:, pair, 0:w].bitcast(F32),
                                          ALU.subtract).then_inc(alo_ready[phase], 1)
                if phase == "ag" and at_step == 1:
                    dve.wait_ge(emptied, read + 4)
                    for j in range(2):
                        c = 2 * g + j
                        dve.wait_ge(sig_ready, c + 1)
                        dve.scalar_tensor_tensor(z[:, c, PAD:PAD + T], t1[:, j, :], bias_in(3 * KS + c),
                                                 t2[:, j, :], ALU.add, ALU.mult).then_inc(z_ready, 1)
                if phase == "cv" and at_step == 1:
                    dve.wait_ge(emptied, read + 4)
                    for j in range(2):
                        c = 2 * g + j
                        dve.wait_ge(c_ready, c + 1)
                        dve.scalar_tensor_tensor(t2[:, j, :], t2[:, j, :], bias_in(2 * KS + c),
                                                 t1[:, j, :], ALU.add, ALU.mult).then_inc(cv_ready, 1)
                        dve.wait_ge(cv_ready, c + 1)
                        for k in range(SCW):
                            src = t2[:, j, META - SCW + 1 + k:META - SCW + 1 + k + SEQ]
                            tap = param("sc_w", k * KS + c)
                            if k == 0:
                                dve.tensor_scalar(cs[:, c, :], src, tap, None, ALU.mult).then_inc(sc_step, 1)
                            else:
                                dve.wait_ge(sc_step, SCW * c + k)
                                dve.scalar_tensor_tensor(cs[:, c, :], src, tap, cs[:, c, :], ALU.mult,
                                                         ALU.add).then_inc(sc_step, 1)
                if phase == "b":
                    tiles = slice(SET * g, SET * (g + 1))
                    if at_step == 0:
                        dve.wait_ge(block_used, ended)
                        dve.tensor_tensor(y_f[:, tiles, :], ps[:, bank:bank + SET, 0:SEQ],
                                          over_two(rstd[:, toks], SEQ, SET), ALU.mult).then_inc(emptied, SET)
                        dve.wait_ge(emptied, read + SET)
                        for c in range(tiles.start, tiles.stop):
                            dve.scalar_tensor_tensor(y_f[:, c, :], y_f[:, c, :], bias_in(c), cs[:, c, :],
                                                     ALU.add, ALU.mult).then_inc(ysc_ready, 1)
                    if at_step == 1:
                        dve.wait_ge(ysc_hi, g + 1)
                        dve.tensor_tensor(y_lo[:, tiles, :], y_f[:, tiles, :], y_hi[:, tiles, :].bitcast(F32),
                                          ALU.subtract).then_inc(ysc_lo, 1)
                if phase in ("down1", "out_sc", "out_cf", "down2"):
                    if at_step == 0:
                        dve.wait_ge(block_used, ended)
                        for j in range(SET):
                            t = SET * g + j
                            dve.scalar_tensor_tensor(res[:, t, toks], ps[:, bank + j, 0:w],
                                                     0.5 if "down" in phase else 1.0, res[:, t, toks],
                                                     ALU.mult, ALU.add).then_inc(emptied, 1)
                    if phase == "out_cf" and at_step == 1:
                        for j in range(SET):
                            norm_operand("gu2", phase, g, j)
                    if "down" in phase and at_step:
                        for j in (0, 1) if at_step == 1 else (2, 3):
                            norm_operand("ag" if phase == "down1" else "down2", phase, g, j)

            def long_conv(q0, q1):
                for q in range(q0, min(q1, CFW * KS)):
                    c, k = divmod(q, CFW)
                    src = z[:, c, k:k + SEQ]
                    if k == 0:
                        dve.wait_ge(z_ready, c + 1)
                        dve.wait_ge(pad_set, 1)
                        dve.tensor_scalar(zc[:, c, :], src, cf_tap(k, c), param("cf_b", c), ALU.mult,
                                          ALU.add).then_inc(cf_step, 1)
                    else:
                        dve.wait_ge(cf_step, q)
                        dve.scalar_tensor_tensor(zc[:, c, :], src, cf_tap(k, c), zc[:, c, :], ALU.mult,
                                                 ALU.add).then_inc(cf_step, 1)
                    if k == CFW - 1:
                        dve.wait_ge(cf_step, q + 1)
                        if c == 0:
                            dve.tensor_copy(ln_sum[:, :], zc[:, 0, :]).then_inc(ln_added, 1)
                        else:
                            dve.wait_ge(ln_added, c)
                            dve.tensor_tensor(ln_sum[:, :], ln_sum[:, :], zc[:, c, :],
                                              ALU.add).then_inc(ln_added, 1)

            def layernorm(b):
                if b == 5:
                    dve.wait_ge(ln_mean_done, 1)
                    dve.tensor_scalar(ln_mu[:, :], ps[:, SET, SEQ:2 * SEQ], 1.0 / DS, None,
                                      ALU.mult).then_inc(ln_mu_set, 1)
                    dve.wait_ge(ln_mu_set, 1)
                    dve.tensor_tensor(zc[:, :, :], zc[:, :, :], over_two(ln_mu[:, :], SEQ, KS),
                                      ALU.subtract).then_inc(centred, 1)
                if b == 7:
                    dve.wait_ge(ln_sq, 1)
                    dve.tensor_reduce(ln_sum[:, :], y_f[:, :, :].rearrange("p c t -> p t c"),
                                      mybir.AxisListType.X, ALU.add).then_inc(ln_var_sum, 1)
                if b == 8:
                    dve.wait_ge(ln_var_done, 1)
                    dve.tensor_scalar(step[:, 0, 0:SEQ], ps[:, 0, SEQ:2 * SEQ], 1.0 / DS, EPS, ALU.mult,
                                      ALU.add).then_inc(ln_var, 1)
                if b == 10:
                    inverse_root(ln_rstd[:, :], step[:, 0, 0:SEQ], step[:, 1, 0:SEQ], ln_mu[:, :],
                                 step[:, 2, 0:SEQ], ln_sd, ln_newton)
                    dve.tensor_tensor(zc[:, :, :], zc[:, :, :], over_two(ln_rstd[:, :], SEQ, KS),
                                      ALU.mult).then_inc(normed, 1)
                if b in (12, 13):
                    half = slice(SET * (b - 12), SET * (b - 11))
                    dve.wait_ge(ycf_hi, b - 11)
                    dve.tensor_tensor(y_lo[:, KS + half.start:KS + half.stop, :], y_f[:, half, :],
                                      y_hi[:, KS + half.start:KS + half.stop, :].bitcast(F32),
                                      ALU.subtract).then_inc(ycf_lo, 1)

            for c in range(KD + 2):
                if c < KD:
                    dve.wait_ge(x_turned, c + 1)
                    dve.tensor_copy(res[:, c, :], ps[:, c % 8, 0:T]).then_inc(emptied, 1)
                if c >= 2:
                    norm_operand("gu1", "start", (c - 2) // SET, (c - 2) % SET)
                    if c % 2 and (c - 2) // 2 in range(1, 1 + RING):
                        low("gu1", 0, (c - 2) // 2 - 1)

            parity_of = [0]

            def phase_blocks(phase, norm=None, between=None):
                def body(g, parity):
                    parity_of[0] = 1 - parity
                    for i in range(n_blocks[phase]):
                        if not (phase == "gu1" and isinstance(g, int) and g == 0 and i < RING):
                            low(phase, g, i)
                        if i in (2, 3, 4):
                            finish(*previous(phase, g), i - 2)
                        if norm and isinstance(g, int) and g == 0 and i == 7:
                            toks = tokens(phase)
                            dve.wait_ge(stats_done[norm], 1)
                            dve.tensor_scalar(step[:, 0, toks], ps[:, 7, 0:width[phase]], 1.0 / D, EPS,
                                              ALU.mult, ALU.add).then_inc(var_ready[norm], 1)
                        if norm and isinstance(g, int) and g == 1 and i == 0:
                            toks = tokens(phase)
                            inverse_root(rstd[:, toks], step[:, 0, toks], step[:, 1, toks], sq[:, 0, toks],
                                         step[:, 2, toks], sd_ready[norm], newton[norm])
                        if between:
                            between(n_blocks[phase] * g + i)
                return body

            def run(phase, norm=None, between=None):
                body = phase_blocks(phase, norm, between)
                n = n_groups[phase]
                if n > SET:
                    body(0, 0)
                    body(1, 1)
                    with dve.Fori(2, n, 2) as g:
                        body(g, 0)
                        body(g + 1, 1)
                else:
                    for g in range(n):
                        body(g, g % 2)

            def conv_from(first, per):
                sums = [first]

                def between(b):
                    long_conv(sums[0], sums[0] + per(b))
                    sums[0] += per(b)
                return between, sums

            run("gu1", "start")
            run("down1")

            def ag_between(b):
                if b == 4:
                    dve.memset(z[:, :, 0:PAD], 0.0).then_inc(pad_set, 1)
                if b >= 12:
                    long_conv(4 * (b - 12), 4 * (b - 11))
            done = 4 * (n_groups["ag"] * N_GU - 12)
            run("ag", "down1", ag_between)
            per_two = 7

            def cv_between(b):
                q = done + b // 2 * per_two + b % 2 * 4
                long_conv(q, q + (3 if b % 2 else 4))
            run("cv", None, cv_between)
            done_cv = done + n_groups["cv"] * N_GU // 2 * per_two

            def b_between(b):
                long_conv(done_cv + 3 * b, done_cv + 3 * b + 3)
            run("b", None, b_between)
            done_b = done_cv + 3 * n_groups["b"] * N_B
            assert CFW * KS - done_b <= 8

            def out_between(b):
                if b < 2:
                    long_conv(done_b + 4 * b, done_b + 4 * b + 4)
                layernorm(b)
            run("out_sc", None, out_between)
            run("out_cf")
            run("gu2", "out_cf")

            def turned_output(b):
                g, i = divmod(b, n_blocks["down2"])
                if g >= 1 and i == 10:
                    dve.wait_ge(o_turned, g)
                    bank = SET * ((g - 1) % 2) + 2
                    dve.tensor_copy(o_tok[:, 1, (g - 1) * 512:g * 512].rearrange("p (j n) -> p j n", n=2 * P),
                                    ps[:, bank:bank + 2, SEQ:2 * SEQ]).then_inc(o_copied_v, 1)
            run("down2", None, turned_output)
            for s in range(3):
                finish("down2", G_D - 1, s)
            dve.wait_ge(stats_done["down2"], 1)
            dve.tensor_scalar(tok[:, 0, :], ps[:, 0, 0:HALVES], 1.0 / D, EPS, ALU.mult,
                              ALU.add).then_inc(var_ready["down2"], 1)
            inverse_root(tok[:, 3, :], tok[:, 0, :], tok[:, 1, :], tok[:, 2, :], tok[:, 3, :],
                         sd_ready["down2"], newton["down2"])
            last = (KD - SET) * P
            dve.wait_ge(o_copied_v, G_D - 1)
            dve.tensor_scalar(o_tok[:, 1, 0:last], o_tok[:, 1, 0:last], tok[:, 3, 1:2], None,
                              ALU.mult).then_inc(o_scaled_v, 1)
            dve.wait_ge(o_turned, G_D)
            dve.tensor_scalar(o_tok[:, 1, last:D].rearrange("p (j n) -> p j n", n=2 * P),
                              ps[:, SET + 2:SET + 4, SEQ:2 * SEQ], tok[:, 3, 1:2], None,
                              ALU.mult).then_inc(o_scaled_v, 1)


_INS = ["x", "meta_tokens", "ffn1_norm", "ffn1_w_gate", "ffn1_w_up", "ffn1_w_down", "mix_norm", "w_in",
        "b_in", "conv_sc_w", "conv_cf_w", "conv_cf_b", "ln_cf_g", "ln_cf_b", "w_out",
        "ffn2_norm", "ffn2_w_gate", "ffn2_w_up", "ffn2_w_down", "final_norm"]


def kernel(**inputs):
    import numpy as np
    import concourse.bacc as bacc
    from concourse.bass_utils import run_bass_kernel_spmd

    nc = bacc.Bacc("TRN2", target_bir_lowering=False, num_devices=1)
    arrays, args = {}, []
    for name in _INS:
        a = np.ascontiguousarray(inputs[name])
        arrays[f"in_{name}"] = a
        args.append(nc.dram_tensor(f"in_{name}", a.shape, mybir.dt.from_np(a.dtype), kind="ExternalInput").ap())
    out = nc.dram_tensor("out_y", inputs["x"].shape, F32, kind="ExternalOutput").ap()
    build(nc, *args, out)
    return run_bass_kernel_spmd(nc, [arrays], core_ids=[0]).results[0]["out_y"]
```

```python
from contextlib import ExitStack

import concourse.bass as bass
from concourse import mybir

ALU = mybir.AluOpType
ACT = mybir.ActivationFunctionType
F32 = mybir.dt.float32
F32R = mybir.dt.float32r

P = 128
EPS = 1e-6
BLOCK = 1024
RING = 4
BANK = 512
SET = 4


def build(nc, x, meta_tokens, ffn1_norm, ffn1_w_gate, ffn1_w_up, ffn1_w_down, mix_norm, w_in, b_in,
          conv_sc_w, conv_cf_w, conv_cf_b, ln_cf_g, ln_cf_b, w_out,
          ffn2_norm, ffn2_w_gate, ffn2_w_up, ffn2_w_down, final_norm, out):
    D = x.shape[2]
    SEQ = x.shape[1]
    META = meta_tokens.shape[0]
    T = META + SEQ
    FF = ffn1_w_gate.shape[2]
    KD = D // P
    KF = FF // P
    DS = conv_sc_w.shape[2]
    KS = DS // P
    SCW = conv_sc_w.shape[1]
    CFW = conv_cf_w.shape[1]
    PAD = CFW - 1 - META
    HALVES = SEQ // P
    ALL = slice(0, T)
    KEPT = slice(META, T)

    G_FF = KF // 2
    G_D = KD // SET
    G_MIX = KS // 2
    G_B = KS // SET
    N_GU = 2 * KD // 4
    N_DOWN = KF // 2
    N_B = KD // 2
    N_OUT = KS // 2

    sizes = [("gu1", G_FF, N_GU), ("down1", G_D, N_DOWN), ("ag", G_MIX, N_GU), ("cv", G_MIX, N_GU),
             ("b", G_B, N_B), ("out_sc", G_D, N_OUT), ("out_cf", G_D, N_OUT),
             ("gu2", G_FF, N_GU), ("down2", G_D, N_DOWN)]
    block0, group0, n_groups, n_blocks = {}, {}, {}, {}
    blocks = groups = 0
    for name, n_g, n_b in sizes:
        block0[name], group0[name], n_groups[name], n_blocks[name] = blocks, groups, n_g, n_b
        blocks += n_g * n_b
        groups += n_g
        assert n_g % 2 == 0 and blocks % RING == 0
    before = {b[0]: a[0] for a, b in zip(sizes, sizes[1:])}

    with ExitStack() as ctx:
        def sb(name, shape, dt=F32):
            return ctx.enter_context(nc.sbuf_tensor(name, shape, dt))

        def sem(name):
            return ctx.enter_context(nc.semaphore(name))

        ps = ctx.enter_context(nc.psum_tensor("ps", [P, 2 * SET, BANK], F32))

        sb("x_region", [P, 2 * KD * T])
        x_at = nc.sbuf_base - 4 * 2 * KD * T
        sb("a_region", [P, 2 * KF * T])
        a_at = nc.sbuf_base - 4 * 2 * KF * T

        raw = [sb(f"raw{i}", [P, BLOCK]) for i in range(RING)]
        w_hi = [sb(f"w_hi{i}", [P, BLOCK], F32R) for i in range(RING)]
        w_lo = [sb(f"w_lo{i}", [P, BLOCK], F32R) for i in range(RING)]
        res = sb("res", [P, KD, T])
        t1 = sb("t1", [P, 2, T])
        t2 = sb("t2", [P, 2, T])
        rstd = sb("rstd", [P, T])
        sq_sum = sb("sq_sum", [P, T])
        sq = sb("sq", [P, 2, T])
        step = sb("step", [P, 3, T])
        par = sb("par", [P, 4, P])
        gain1 = sb("gain1", [P, KD])
        ident = sb("ident", [P, P])
        ones = sb("ones", [P, P])
        tok = sb("tok", [P, 4, HALVES])

        def at(name, offset, shape, dt=F32):
            return nc.alloc_sbuf_tensor_at(name, shape, dt, offset=offset)

        x_hi = at("x_hi", x_at, [P, KD, T], F32R)
        x_lo = at("x_lo", x_at + 4 * KD * T, [P, KD, T], F32R)
        o_tile = at("o_tile", x_at, [P, SET, SEQ])
        o_tok = at("o_tok", x_at + 4 * SET * SEQ, [P, HALVES, D])
        a_hi = at("a_hi", a_at, [P, KF, T], F32R)
        a_lo = at("a_lo", a_at + 4 * KF * T, [P, KF, T], F32R)
        x_tok = at("x_tok", a_at, [P, HALVES, D])
        m_tok = at("m_tok", a_at + 4 * HALVES * D, [P, D])
        par_rows = at("par_rows", a_at + 4 * (HALVES + 1) * D, [P, 4, P])
        gain_rows = at("gain_rows", a_at + 4 * (HALVES + 1) * D + 16 * P, [KD, P])
        tile_bytes = 4 * SEQ
        y_hi = at("y_hi", a_at, [P, 2 * KS, SEQ], F32R)
        y_lo = at("y_lo", a_at + 2 * KS * tile_bytes, [P, 2 * KS, SEQ], F32R)
        y_f = at("y_f", a_at + 4 * KS * tile_bytes, [P, KS, SEQ])
        cs = at("cs", a_at + 5 * KS * tile_bytes, [P, KS, SEQ])
        zc = at("zc", a_at + 6 * KS * tile_bytes, [P, KS, SEQ])
        z = at("z", a_at + 7 * KS * tile_bytes, [P, KS, PAD + T])
        ln_at = a_at + 7 * KS * tile_bytes + 4 * KS * (PAD + T)
        ln_sum = at("ln_sum", ln_at, [P, SEQ])
        ln_mu = at("ln_mu", ln_at + tile_bytes, [P, SEQ])
        ln_rstd = at("ln_rstd", ln_at + 2 * tile_bytes, [P, SEQ])
        zd = at("zd", ln_at + 3 * tile_bytes, [P, 2, SEQ])
        PRODUCTS = 6
        tap_product = at("tap_product", ln_at + 5 * tile_bytes, [P, PRODUCTS, 2, SEQ])
        assert ln_at + (5 + 2 * PRODUCTS) * tile_bytes <= a_at + 4 * 2 * KF * T

        rows0 = [("mix", mix_norm[0], KD), ("ffn2", ffn2_norm[0], KD),
                 ("final", final_norm, KD), ("cf_b", conv_cf_b[0], KS), ("ln_g", ln_cf_g[0], KS),
                 ("ln_b", ln_cf_b[0], KS)]
        row0, used = {}, 0
        for name, _, n in rows0:
            row0[name] = used
            used += n
        row0["sc_w"] = used
        n_rows = [used + SCW * KS, b_in.shape[1] // P, P, CFW * KS - P]

        def param(name, i):
            if name == "ffn1":
                return gain1[:, i:i + 1]
            return par[:, 0, row0[name] + i:row0[name] + i + 1]

        def bias_in(i):
            return par[:, 1, i:i + 1]

        def cf_tap(k, c):
            row = k * KS + c
            return par[:, 2 + row // P, row % P:row % P + 1]

        raw_loaded = [sem(f"raw_loaded{i}") for i in range(RING)]
        hi_ready = sem("hi_ready")
        lo_ready = sem("lo_ready")
        block_used = sem("block_used")
        emptied = sem("emptied")
        gain_loaded, gain_turned, gain_ready = sem("gain_loaded"), sem("gain_turned"), sem("gain_ready")
        par_loaded, x_loaded = sem("par_loaded"), [sem(f"x_loaded{i}") for i in range(5)]
        ones_set, ident_zero, ident_set = sem("ones_set"), sem("ident_zero"), sem("ident_set")
        par_turned, par_ready, x_turned = sem("par_turned"), sem("par_ready"), sem("x_turned")
        gain_of = {"start": "ffn1", "down1": "mix", "out_cf": "ffn2", "down2": "final"}
        xhi_ready, xlo_ready, sq_ready, sum_ready, stats_done, var_ready, sd_ready, newton = (
            {n: sem(f"{what}_{n}") for n in gain_of}
            for what in ("xhi_ready", "xlo_ready", "sq_ready", "sum_ready", "stats_done", "var_ready",
                         "sd_ready", "newton"))
        silu_ready, prod_ready, ahi_ready, alo_ready = (
            {n: sem(f"{what}_{n}") for n in ("gu1", "gu2")}
            for what in ("silu_ready", "prod_ready", "ahi_ready", "alo_ready"))
        pad_set, sig_ready, z_ready = sem("pad_set"), sem("sig_ready"), sem("z_ready")
        c_ready, cv_ready, sc_step = sem("c_ready"), sem("cv_ready"), sem("sc_step")
        cf_step, ln_added = sem("cf_step"), sem("ln_added")
        cf_first, cf_second, cf_product = sem("cf_first"), sem("cf_second"), sem("cf_product")
        sc_first = sem("sc_first")
        tile_done = sem("tile_done")
        ysc_ready, ysc_hi, ysc_lo = sem("ysc_ready"), sem("ysc_hi"), sem("ysc_lo")
        ln_mean_done, ln_mu_set, centred = sem("ln_mean_done"), sem("ln_mu_set"), sem("centred")
        ln_sq, ln_var_sum, ln_var_done = sem("ln_sq"), sem("ln_var_sum"), sem("ln_var_done")
        ln_var, ln_sd, ln_newton, normed = sem("ln_var"), sem("ln_sd"), sem("ln_newton"), sem("normed")
        ycf_ready, ycf_hi, ycf_lo = sem("ycf_ready"), sem("ycf_hi"), sem("ycf_lo")
        o_turned, o_copied_s, o_copied_v = sem("o_turned"), sem("o_copied_s"), sem("o_copied_v")
        o_scaled_s, o_scaled_v, stored = sem("o_scaled_s"), sem("o_scaled_v"), sem("stored")

        def before_block(phase, g, i):
            return block0[phase] + i + n_blocks[phase] * g

        def slot(phase, g, i):
            return (n_blocks[phase] * g + i) % RING if isinstance(g, int) else i % RING

        def turn(phase, g, i):
            if isinstance(g, int):
                return (block0[phase] + n_blocks[phase] * g + i) // RING
            return (block0[phase] + i) // RING + n_blocks[phase] // RING * g

        def banks_before(phase, g):
            return KD + SET * group0[phase] + SET * g

        def previous(phase, g):
            if not isinstance(g, int) or g > 0:
                return phase, g - 1
            return (before[phase], n_groups[before[phase]] - 1) if phase in before else ("", 0)

        def over_groups(engine, phase, body):
            n = n_groups[phase]
            body(0, 0)
            if n > SET:
                with engine.Fori(1, n - 1, 2) as g:
                    body(g, 1)
                    body(g + 1, 0)
            else:
                for g in range(1, n - 1):
                    body(g, g % 2)
            if n > 1:
                body(n - 1, 1)

        width = {"gu1": T, "down1": T, "ag": T, "cv": T, "b": SEQ, "out_sc": SEQ, "out_cf": SEQ,
                 "gu2": SEQ, "down2": SEQ}

        def tokens(phase):
            return slice(0, T) if width[phase] == T else slice(META, T)

        STEPS = CFW - 1
        spread = {"ag": [0] * (N_GU + 6) + [3, 2] + [2, 2, 1, 2, 2, 2, 2, 2] * (G_MIX - 2),
                  "cv": [2, 2, 1, 1, 2, 2, 2, 2] * G_MIX,
                  "b": [2, 1, 0, 1, 2, 2, 2, 2] * G_B,
                  "out_sc": [0, 0, 1, 3, 4, 3]}
        first_step, steps_left = {}, STEPS * KS // 2
        for name in spread:
            first_step[name] = STEPS * KS // 2 - steps_left
            steps_left = max(0, steps_left - sum(spread[name]))
        assert steps_left == 0

        def steps_after(phase, b):
            if phase not in spread or b >= len(spread[phase]):
                return []
            q = first_step[phase] + sum(spread[phase][:b])
            return [(*divmod(i, STEPS), i) for i in range(q, min(q + spread[phase][b], STEPS * KS // 2))]

        out_pieces = [slice(g * BANK, (g + 1) * BANK) for g in range(G_D)]

        block = ctx.enter_context(nc.Block())

        @block.sync
        def _(sp):
            def load_x(i):
                cols = slice(i * (D // 4), (i + 1) * (D // 4))
                sp.dma_start(x_tok[:, :, cols],
                             x[0, :, cols].rearrange("(h p) d -> p h d", p=P)).then_inc(x_loaded[i], 16)

            def load(phase, g, i, src, n):
                ahead, s = before_block(phase, g, i), slot(phase, g, i)
                if not isinstance(ahead, int) or ahead >= RING:
                    sp.wait_ge(lo_ready, ahead - (RING - 1))
                sp.dma_start(raw[s][:, :].rearrange("p (c n) -> p c n", n=n), src).then_inc(raw_loaded[s], 16)

            def paired(phase, wa, wb, col_a, col_b):
                rows = [w.rearrange("(q c p) n -> q p c n", c=4, p=P) for w in (wa, wb)]

                def body(g, parity):
                    for i in range(n_blocks[phase]):
                        if phase == "gu1" and isinstance(g, int) and g == 0 and i < 4:
                            load_x(i)
                        src = rows[i % 2][i // 2, :, :, bass.ds(g * 256 + (col_a, col_b)[i % 2], 256)]
                        load(phase, g, i, src, 256)
                over_groups(sp, phase, body)

            def single(phase, w, first_row):
                rows = w.rearrange("(k c p) n -> k p c n", c=2, p=P)

                def body(g, parity):
                    for i in range(n_blocks[phase]):
                        load(phase, g, i, rows[first_row // (2 * P) + i, :, :, bass.ds(g * 512, 512)], 512)
                over_groups(sp, phase, body)

            paired("gu1", ffn1_w_gate[0], ffn1_w_up[0], 0, 0)
            single("down1", ffn1_w_down[0], 0)
            paired("ag", w_in[0], w_in[0], 3 * DS, 4 * DS)
            paired("cv", w_in[0], w_in[0], DS, 2 * DS)
            single("b", w_in[0], 0)
            single("out_sc", w_out[0], 0)
            single("out_cf", w_out[0], DS)
            paired("gu2", ffn2_w_gate[0], ffn2_w_up[0], 0, 0)
            single("down2", ffn2_w_down[0], 0)

            for i, cols in enumerate(out_pieces):
                sp.wait_ge(o_scaled_s, i + 1)
                sp.dma_start(out[0, 0:P, cols], o_tok[:, 0, cols]).then_inc(stored, 16)
                sp.wait_ge(o_scaled_v, i + 1)
                sp.dma_start(out[0, P:2 * P, cols], o_tok[:, 1, cols]).then_inc(stored, 16)
            sp.wait_ge(stored, 32 * len(out_pieces))

        @block.gpsimd
        def _(pool):
            pool.memset(ident[:, :], 0.0).then_inc(ident_zero, 1)
            pool.wait_ge(ident_zero, 1)
            pool.affine_select(out=ident[:, :], in_=ident[:, :], compare_op=ALU.not_equal, fill=1.0, base=0,
                               pattern=[[-1, P]], channel_multiplier=1).then_inc(ident_set, 1)
            for name, src, n in rows0:
                pool.dma_start(par_rows[row0[name]:row0[name] + n, 0, :],
                               src.rearrange("(r p) -> r p", p=P)).then_inc(par_loaded, 16)
            pool.dma_start(par_rows[row0["sc_w"]:n_rows[0], 0, :],
                           conv_sc_w[0].rearrange("k (c p) -> (k c) p", p=P)).then_inc(par_loaded, 16)
            pool.dma_start(par_rows[0:n_rows[1], 1, :],
                           b_in[0].rearrange("(r p) -> r p", p=P)).then_inc(par_loaded, 16)
            taps = conv_cf_w[0].rearrange("k (c p) -> (k c) p", p=P)
            pool.dma_start(par_rows[0:P, 2, :], taps[0:P, :]).then_inc(par_loaded, 16)
            pool.dma_start(par_rows[0:n_rows[3], 3, :], taps[P:P + n_rows[3], :]).then_inc(par_loaded, 16)

        @block.tensor
        def _(pe):
            def turn_x(c, bank):
                cols = slice(c * P, (c + 1) * P)
                pe.transpose(ps[:, bank, 0:META], m_tok[0:META, cols], ident[0:META, 0:META])
                for h in range(HALVES):
                    m = pe.transpose(ps[:, bank, META + h * P:META + (h + 1) * P], x_tok[:, h, cols], ident[:, :])
                m.then_inc(x_turned, 1)

            def start_between(i):
                if i == 1:
                    pe.wait_ge(par_loaded, 16 * (len(rows0) + 4))
                    pe.wait_ge(emptied, 5)
                    for s in range(4):
                        pe.transpose(ps[:, 4, s * P:s * P + n_rows[s]], par_rows[0:n_rows[s], s, :],
                                     ident[0:n_rows[s], 0:n_rows[s]]).then_inc(par_turned, 1)
                    for c in (8, 9, 10, 11):
                        if c == 8:
                            pe.wait_ge(x_loaded[2], 16)
                        if c == 11:
                            pe.wait_ge(par_ready, 4)
                        else:
                            pe.wait_ge(emptied, c - 2)
                        turn_x(c, 4 + (c - 7) % 4)
                if i == 3:
                    pe.wait_ge(x_loaded[3], 16)
                    for c in (12, 13, 14, 15):
                        pe.wait_ge(emptied, c - 3)
                        turn_x(c, 4 + (c - 7) % 4)

            pe.wait_ge(ident_set, 1)
            pe.wait_ge(gain_loaded, 16)
            pe.transpose(ps[:, 7, 0:KD], gain_rows[:, :], ident[0:KD, 0:KD]).then_inc(gain_turned, 1)
            pe.wait_ge(x_loaded[4], 16)
            for c in range(8):
                if c % 4 == 0:
                    pe.wait_ge(x_loaded[c // 4], 16)
                if c == 7:
                    pe.wait_ge(gain_ready, 1)
                turn_x(c, c)

            def product(bank, n, w_high, w_low, act_high, act_low, first, last):
                dst = ps[:, bank, 0:n]
                pe.matmul(dst, w_high, act_high, start=first, stop=False)
                pe.matmul(dst, w_high, act_low, start=False, stop=False)
                return pe.matmul(dst, w_low, act_high, start=False, stop=last)

            def start_group(phase, g):
                if phase == "gu1" and isinstance(g, int) and g == 0:
                    pe.wait_ge(emptied, SET)
                else:
                    pe.wait_ge(emptied, banks_before(phase, g) - SET)

            def start_block(phase, g, i):
                pe.wait_ge(lo_ready, before_block(phase, g, i) + 1)

            def square_sums(norm, phase):
                pe.wait_ge(sum_ready[norm], KD)
                pe.matmul(ps[:, 7, 0:width[phase]], ones[:, :], sq_sum[:, tokens(phase)],
                          start=True, stop=True).then_inc(stats_done[norm], 1)

            def paired(phase, norm):
                toks = tokens(phase)

                def body(g, parity):
                    first_group = isinstance(g, int) and g == 0
                    start_group(phase, g)
                    if norm and isinstance(g, int) and g == 1:
                        pe.wait_ge(var_ready[norm], 1)
                    for i in range(n_blocks[phase]):
                        s = slot(phase, g, i)
                        start_block(phase, g, i)
                        for j in range(2):
                            for c in range(4):
                                k = 4 * (i // 2) + c
                                if norm and first_group and i % 2 == 0 and j == 0:
                                    pe.wait_ge(xlo_ready[norm], k + 1)
                                cols = slice(c * 256 + j * P, c * 256 + (j + 1) * P)
                                m = product(SET * parity + 2 * (i % 2) + j, width[phase],
                                            w_hi[s][:, cols], w_lo[s][:, cols],
                                            x_hi[:, k, toks], x_lo[:, k, toks], k == 0, k == KD - 1)
                        m.then_inc(block_used, 1)
                        if norm and first_group and i == (5 if norm == "start" else 3):
                            square_sums(norm, phase)
                        if norm == "start" and first_group:
                            start_between(i)
                over_groups(pe, phase, body)

            def single_group(phase, g, parity, high, low, first_k, toks, n_k, ready, per_block, extra=None):
                start_group(phase, g)
                for i in range(n_blocks[phase]):
                    s = slot(phase, g, i) if isinstance(g, int) else (n_blocks[phase] * parity + i) % RING
                    start_block(phase, g, i)
                    if ready is not None and isinstance(g, int) and g == 0:
                        pe.wait_ge(ready, per_block(i))
                    for j in range(SET):
                        for c in range(2):
                            k = 2 * i + c
                            cols = slice(c * 512 + j * P, c * 512 + (j + 1) * P)
                            m = product(SET * parity + j, width[phase], w_hi[s][:, cols], w_lo[s][:, cols],
                                        high[:, first_k + k, toks], low[:, first_k + k, toks],
                                        k == 0, k == n_k - 1)
                        if phase == "down2" and g == G_D - 1 and i == n_blocks[phase] - 1 and j < SET - 1:
                            m.then_inc(tile_done, 1)
                    m.then_inc(block_used, 1)
                    if extra:
                        extra(n_blocks[phase] * g + i)

            def down(phase, gate_up, extra=None):
                for g in range(G_D):
                    single_group(phase, g, g % 2, a_hi, a_lo, 0, slice(0, width[phase]), KF,
                                 alo_ready[gate_up], lambda i: i + 1, extra)

            def layernorm_sums(b):
                if b == 5:
                    pe.wait_ge(ln_added, KS)
                    pe.wait_ge(emptied, banks_before("out_sc", 1))
                    pe.matmul(ps[:, 0, SEQ:2 * SEQ], ones[:, :], ln_sum[:, :],
                              start=True, stop=True).then_inc(ln_mean_done, 1)
                if b == 9:
                    pe.wait_ge(ln_var_sum, 1)
                    pe.wait_ge(emptied, banks_before("out_sc", 2))
                    pe.matmul(ps[:, SET, SEQ:2 * SEQ], ones[:, :], ln_sum[:, :],
                              start=True, stop=True).then_inc(ln_var_done, 1)
                if b == 7:
                    pe.wait_ge(ln_mu_set, 1)
                if b == 11:
                    pe.wait_ge(ln_var, 1)

            def turn_output(g):
                pe.wait_ge(xhi_ready["down2"], SET * (g + 1))
                for j in range(SET):
                    for h in range(HALVES):
                        at_col = SEQ + (j % 2) * P
                        m = pe.transpose(ps[:, SET * (g % 2) + 2 * h + j // 2, at_col:at_col + P],
                                         o_tile[:, j, h * P:(h + 1) * P], ident[:, :])
                m.then_inc(o_turned, 1)

            def output_between(b):
                g, i = divmod(b, n_blocks["down2"])
                if g >= 1 and i == 6:
                    turn_output(g - 1)
                if g >= 1 and i == n_blocks["down2"] - 1:
                    pe.wait_ge(o_copied_s, g)
                    pe.wait_ge(o_copied_v, g)

            pe.wait_ge(ones_set, 1)
            paired("gu1", "start")
            down("down1", "gu1")
            paired("ag", "down1")
            paired("cv", None)
            for g in range(G_B):
                single_group("b", g, g % 2, x_hi, x_lo, 0, tokens("b"), KD, None, None)
            for g in range(G_D):
                single_group("out_sc", g, g % 2, y_hi, y_lo, 0, slice(0, SEQ), KS,
                             ysc_lo, lambda i: i // 2 + 1, layernorm_sums)
            for g in range(G_D):
                single_group("out_cf", g, g % 2, y_hi, y_lo, KS, slice(0, SEQ), KS,
                             ycf_lo, lambda i: i // 2 + 1)
            paired("gu2", "out_cf")
            down("down2", "gu2", output_between)
            turn_output(G_D - 1)
            pe.wait_ge(sum_ready["down2"], KD)
            for h in range(HALVES):
                m = pe.matmul(ps[:, 0, h:h + 1], sq_sum[:, META + h * P:META + (h + 1) * P], ones[:, 0:1],
                              start=True, stop=True)
            m.then_inc(stats_done["down2"], 1)

        @block.scalar
        def _(act):
            act.dma_start(gain_rows[0:KD, :], ffn1_norm[0].rearrange("(r p) -> r p", p=P)).then_inc(gain_loaded, 16)
            act.dma_start(m_tok[0:META, :], meta_tokens).then_inc(x_loaded[4], 16)

            def high(phase, g, i):
                s = slot(phase, g, i)
                act.wait_ge(raw_loaded[s], 16 * turn(phase, g, i) + 16)
                ahead = before_block(phase, g, i)
                if not isinstance(ahead, int) or ahead >= RING:
                    act.wait_ge(block_used, ahead - (RING - 1))
                act.activation(w_hi[s][:, :], raw[s][:, :], ACT.Copy).then_inc(hi_ready, 1)

            def operand(phase, norm, t):
                toks = tokens(phase)
                act.wait_ge(emptied, t + 1 if norm == "start" else banks_before(norm, 0) + t + 1)
                dst = x_hi[:, t, toks]
                if norm == "down2":
                    if t >= SET and t % SET == 0:
                        act.wait_ge(o_turned, t // SET)
                    dst = o_tile[:, t % SET, :]
                act.activation(dst, res[:, t, toks], ACT.Copy,
                               scale=param(gain_of[norm], t)).then_inc(xhi_ready[norm], 1)

            def square(phase, norm, t):
                toks = tokens(phase)
                if t >= 2:
                    act.wait_ge(sum_ready[norm], t - 1)
                act.activation(sq[:, t % 2, toks], res[:, t, toks], ACT.Square).then_inc(sq_ready[norm], 1)

            def root(norm, phase):
                act.wait_ge(var_ready[norm], 1)
                act.activation(step[:, 1, tokens(phase)], step[:, 0, tokens(phase)],
                               ACT.Sqrt).then_inc(sd_ready[norm], 1)

            def finish(now, phase, g, at_step):
                read = banks_before(phase, g) if phase else 0
                if phase in ("gu1", "gu2"):
                    w = width[phase]
                    if at_step == 0:
                        act.wait_ge(emptied, read + 2)
                        act.activation(t1[:, :, 0:w], t1[:, :, 0:w], ACT.Silu).then_inc(silu_ready[phase], 1)
                    if at_step == 1:
                        act.wait_ge(prod_ready[phase], g + 1)
                        act.activation(a_hi[:, bass.ds(2 * g, 2), 0:w], t2[:, :, 0:w],
                                       ACT.Copy).then_inc(ahi_ready[phase], 1)
                if phase in ("down1", "down2") and at_step < 2:
                    for j in (0, 1) if at_step == 0 else (2, 3):
                        operand("ag" if phase == "down1" else "down2", phase, SET * g + j)
                        square("ag" if phase == "down1" else "down2", phase, SET * g + j)
                if phase == "out_cf" and at_step == 0:
                    for j in range(SET):
                        operand("gu2", phase, SET * g + j)
                        square("gu2", phase, SET * g + j)
                if phase == "ag" and at_step == 0:
                    act.wait_ge(emptied, read + 4)
                    for j in range(2):
                        act.activation(t2[:, j, :], t2[:, j, :], ACT.Sigmoid,
                                       bias=bias_in(4 * KS + 2 * g + j)).then_inc(sig_ready, 1)
                if phase == "cv" and at_step == 0:
                    act.wait_ge(emptied, read + 2)
                    for j in range(2):
                        act.activation(t1[:, j, :], t1[:, j, :], ACT.Identity,
                                       bias=bias_in(KS + 2 * g + j)).then_inc(c_ready, 1)
                if phase == "cv" and at_step == 1:
                    for c in (2 * g, 2 * g + 1):
                        act.wait_ge(cv_ready, c + 1)
                        act.activation(cs[:, c, :], t2[:, c % 2, META - SCW + 1:META - SCW + 1 + SEQ], ACT.Copy,
                                       scale=param("sc_w", c)).then_inc(sc_first, 1)
                if phase == "ag" and at_step == 2:
                    act.wait_ge(pad_set, 1)
                    for c in (2 * g, 2 * g + 1):
                        act.wait_ge(z_ready, c + 1)
                        act.activation(zc[:, c, :], z[:, c, 0:SEQ], ACT.Identity, scale=cf_tap(0, c),
                                       bias=param("cf_b", c)).then_inc(cf_first, 1)
                if phase == "b" and at_step == 0:
                    act.wait_ge(ysc_ready, SET * (g + 1))
                    act.activation(y_hi[:, SET * g:SET * (g + 1), :], y_f[:, SET * g:SET * (g + 1), :],
                                   ACT.Copy).then_inc(ysc_hi, 1)

            def conv_products(phase, b):
                for pair, n, q in steps_after(phase, b):
                    tiles = (2 * pair, 2 * pair + 1)
                    if n == 0:
                        act.wait_ge(z_ready, tiles[1] + 1)
                        if pair:
                            act.wait_ge(cf_step, STEPS * pair)
                        for c in tiles:
                            act.activation(zd[:, c % 2, :], z[:, c, 1:1 + SEQ], ACT.Copy,
                                           scale=cf_tap(1, c)).then_inc(cf_second, 1)
                    if n < STEPS - 1:
                        if q >= PRODUCTS:
                            act.wait_ge(cf_step, q - PRODUCTS + 1)
                        for c in tiles:
                            act.activation(tap_product[:, q % PRODUCTS, c % 2, :], z[:, c, 2 + n:2 + n + SEQ],
                                           ACT.Copy, scale=cf_tap(2 + n, c)).then_inc(cf_product, 1)

            def layernorm(b):
                if b == 9:
                    act.wait_ge(centred, 1)
                    act.wait_ge(ysc_lo, G_B)
                    act.activation(y_f[:, :, :], zc[:, :, :], ACT.Square).then_inc(ln_sq, 1)
                if b == 12:
                    act.wait_ge(ln_var, 1)
                    act.activation(step[:, 1, 0:SEQ], step[:, 0, 0:SEQ], ACT.Sqrt).then_inc(ln_sd, 1)
                if b in (14, 15):
                    half = slice(SET * (b - 14), SET * (b - 13))
                    act.wait_ge(normed, 1)
                    for c in range(half.start, half.stop):
                        act.activation(y_f[:, c, :], zc[:, c, :], ACT.Silu, scale=param("ln_g", c),
                                       bias=param("ln_b", c)).then_inc(ycf_ready, 1)
                    act.wait_ge(ycf_ready, half.stop)
                    act.activation(y_hi[:, KS + half.start:KS + half.stop, :], y_f[:, half, :],
                                   ACT.Copy).then_inc(ycf_hi, 1)

            act.wait_ge(gain_turned, 1)
            act.activation(gain1[:, :], ps[:, 7, 0:KD], ACT.Copy).then_inc(gain_ready, 1)
            act.wait_ge(gain_ready, 1)
            for q in range(4):
                for t in range(4 * q, 4 * q + 4):
                    operand("gu1", "start", t)
                for i in (2 * q, 2 * q + 1):
                    high("gu1", 0, i)
                for t in range(4 * q, 4 * q + 4):
                    square("gu1", "start", t)
                if q == 1:
                    act.wait_ge(par_turned, 4)
                    for s in range(4):
                        act.activation(par[:, s, 0:n_rows[s]], ps[:, 4, s * P:s * P + n_rows[s]],
                                       ACT.Copy).then_inc(par_ready, 1)
            act.wait_ge(par_ready, 4)

            def phase_blocks(phase, norm=None, between=None):
                def body(g, parity):
                    for i in range(n_blocks[phase]):
                        if not (phase == "gu1" and isinstance(g, int) and g == 0):
                            high(phase, g, i)
                        if i in (3, 4, 5):
                            finish(phase, *previous(phase, g), i - 3)
                        if norm and isinstance(g, int) and g == 0 and i == 7:
                            root(norm, phase)
                        if phase in spread:
                            conv_products(phase, n_blocks[phase] * g + i)
                        if between:
                            between(n_blocks[phase] * g + i)
                over_groups(act, phase, body)

            def turned_output(b):
                g, i = divmod(b, n_blocks["down2"])
                if g >= 1 and i == 10:
                    act.wait_ge(o_turned, g)
                    bank = SET * ((g - 1) % 2)
                    act.activation(o_tok[:, 0, (g - 1) * 512:g * 512].rearrange("p (j n) -> p j n", n=2 * P),
                                   ps[:, bank:bank + 2, SEQ:2 * SEQ],
                                   ACT.Copy).then_inc(o_copied_s, 1)

            phase_blocks("gu1", "start")
            phase_blocks("down1")
            phase_blocks("ag", "down1")
            phase_blocks("cv")
            phase_blocks("b")
            phase_blocks("out_sc", None, layernorm)
            phase_blocks("out_cf")
            phase_blocks("gu2", "out_cf")
            phase_blocks("down2", None, turned_output)
            act.activation(step[:, 1, 0:1], step[:, 0, 0:1], ACT.Sqrt)
            for t in range(KD - SET, KD):
                act.wait_ge(emptied, banks_before("down2", 0) + t + 1)
                square("down2", "down2", t)
            for t in range(KD - SET, KD):
                operand("down2", "down2", t)
            act.wait_ge(var_ready["down2"], 1)
            act.activation(tok[:, 1, :], tok[:, 0, :], ACT.Sqrt).then_inc(sd_ready["down2"], 1)
            act.wait_ge(newton["down2"], 5)
            act.wait_ge(o_copied_s, G_D - 1)
            for cols in out_pieces:
                if cols.stop < D:
                    act.activation(o_tok[:, 0, cols], o_tok[:, 0, cols], ACT.Copy,
                                   scale=tok[:, 3, 0:1]).then_inc(o_scaled_s, 1)
            act.wait_ge(o_turned, G_D)
            act.activation(o_tok[:, 0, cols].rearrange("p (j n) -> p j n", n=2 * P),
                           ps[:, SET:SET + 2, SEQ:2 * SEQ], ACT.Copy,
                           scale=tok[:, 3, 0:1]).then_inc(o_scaled_s, 1)

        @block.vector
        def _(dve):
            dve.memset(ones[:, :], 1.0).then_inc(ones_set, 1)

            def low(phase, g, i):
                s = slot(phase, g, i)
                dve.wait_ge(hi_ready, before_block(phase, g, i) + 1)
                dve.tensor_tensor(w_lo[s][:, :], raw[s][:, :], w_hi[s][:, :].bitcast(F32),
                                  ALU.subtract).then_inc(lo_ready, 1)

            def operand(phase, norm, t):
                toks = tokens(phase)
                if norm != "down2":
                    dve.wait_ge(xhi_ready[norm], t + 1)
                    dve.scalar_tensor_tensor(x_lo[:, t, toks], res[:, t, toks], param(gain_of[norm], t),
                                             x_hi[:, t, toks].bitcast(F32), ALU.mult,
                                             ALU.subtract).then_inc(xlo_ready[norm], 1)

            def add_square(phase, norm, t):
                toks = tokens(phase)
                dve.wait_ge(sq_ready[norm], t + 1)
                if t == 0:
                    dve.tensor_copy(sq_sum[:, toks], sq[:, 0, toks]).then_inc(sum_ready[norm], 1)
                else:
                    dve.wait_ge(sum_ready[norm], t)
                    dve.tensor_tensor(sq_sum[:, toks], sq_sum[:, toks], sq[:, t % 2, toks],
                                      ALU.add).then_inc(sum_ready[norm], 1)

            def inverse_root(dst, var, sd, y, q, sd_done, steps):
                dve.wait_ge(sd_done, 1)
                dve.reciprocal(y, sd).then_inc(steps, 1)
                dve.wait_ge(steps, 1)
                dve.tensor_tensor(q, var, y, ALU.mult).then_inc(steps, 1)
                dve.wait_ge(steps, 2)
                dve.tensor_tensor(q, q, y, ALU.mult).then_inc(steps, 1)
                dve.wait_ge(steps, 3)
                dve.tensor_scalar(q, q, -0.5, 1.5, ALU.mult, ALU.add).then_inc(steps, 1)
                dve.wait_ge(steps, 4)
                dve.tensor_tensor(dst, q, y, ALU.mult).then_inc(steps, 1)
                dve.wait_ge(steps, 5)

            def over_two(row, w, n=2):
                return row.unsqueeze(1).broadcast_to([P, n, w])

            def finish(phase, g, at_step):
                if not phase:
                    return
                bank = SET * ((g if isinstance(g, int) else parity_of[0]) % 2)
                w, toks = width[phase], tokens(phase)
                read = banks_before(phase, g)
                ended = before_block(phase, g, n_blocks[phase])
                if phase in ("gu1", "gu2", "ag", "cv"):
                    if at_step == 0:
                        factor = over_two(rstd[:, toks], w)
                        dve.wait_ge(block_used, ended)
                        dve.tensor_tensor(t1[:, :, 0:w], ps[:, bank:bank + 2, 0:w], factor,
                                          ALU.mult).then_inc(emptied, 2)
                        dve.tensor_tensor(t2[:, :, 0:w], ps[:, bank + 2:bank + 4, 0:w], factor,
                                          ALU.mult).then_inc(emptied, 2)
                if phase in ("gu1", "gu2"):
                    if at_step == 1:
                        dve.wait_ge(silu_ready[phase], g + 1)
                        dve.wait_ge(emptied, read + 4)
                        dve.tensor_tensor(t2[:, :, 0:w], t1[:, :, 0:w], t2[:, :, 0:w],
                                          ALU.mult).then_inc(prod_ready[phase], 1)
                    if at_step == 2:
                        dve.wait_ge(ahi_ready[phase], g + 1)
                        pair = bass.ds(2 * g, 2)
                        dve.tensor_tensor(a_lo[:, pair, 0:w], t2[:, :, 0:w], a_hi[:, pair, 0:w].bitcast(F32),
                                          ALU.subtract).then_inc(alo_ready[phase], 1)
                if phase == "ag" and at_step == 1:
                    dve.wait_ge(emptied, read + 4)
                    for j in range(2):
                        c = 2 * g + j
                        dve.wait_ge(sig_ready, c + 1)
                        dve.scalar_tensor_tensor(z[:, c, PAD:PAD + T], t1[:, j, :], bias_in(3 * KS + c),
                                                 t2[:, j, :], ALU.add, ALU.mult).then_inc(z_ready, 1)
                if phase == "cv" and at_step == 1:
                    dve.wait_ge(emptied, read + 4)
                    for j in range(2):
                        c = 2 * g + j
                        dve.wait_ge(c_ready, c + 1)
                        dve.scalar_tensor_tensor(t2[:, j, :], t2[:, j, :], bias_in(2 * KS + c),
                                                 t1[:, j, :], ALU.add, ALU.mult).then_inc(cv_ready, 1)
                if phase == "cv" and at_step == 2:
                    dve.wait_ge(sc_first, 2 * (g + 1))
                    for k in range(1, SCW):
                        for c in (2 * g, 2 * g + 1):
                            if k > 1:
                                dve.wait_ge(sc_step, (SCW - 1) * 2 * g + 2 * (k - 2) + c % 2 + 1)
                            off = META - SCW + 1 + k
                            dve.scalar_tensor_tensor(cs[:, c, :], t2[:, c % 2, off:off + SEQ],
                                                     param("sc_w", k * KS + c), cs[:, c, :], ALU.mult,
                                                     ALU.add).then_inc(sc_step, 1)
                if phase == "b":
                    tiles = slice(SET * g, SET * (g + 1))
                    if at_step == 0:
                        dve.wait_ge(block_used, ended)
                        dve.tensor_tensor(y_f[:, tiles, :], ps[:, bank:bank + SET, 0:SEQ],
                                          over_two(rstd[:, toks], SEQ, SET), ALU.mult).then_inc(emptied, SET)
                        dve.wait_ge(emptied, read + SET)
                        for c in range(tiles.start, tiles.stop):
                            dve.scalar_tensor_tensor(y_f[:, c, :], y_f[:, c, :], bias_in(c), cs[:, c, :],
                                                     ALU.add, ALU.mult).then_inc(ysc_ready, 1)
                    if at_step == 1:
                        dve.wait_ge(ysc_hi, g + 1)
                        dve.tensor_tensor(y_lo[:, tiles, :], y_f[:, tiles, :], y_hi[:, tiles, :].bitcast(F32),
                                          ALU.subtract).then_inc(ysc_lo, 1)
                if phase in ("down1", "out_sc", "out_cf", "down2"):
                    if at_step == 0:
                        very_last = phase == "down2" and g == G_D - 1
                        if not very_last:
                            dve.wait_ge(block_used, ended)
                        for j in range(SET):
                            if very_last and j < SET - 1:
                                dve.wait_ge(tile_done, j + 1)
                            elif very_last:
                                dve.wait_ge(block_used, ended)
                            t = SET * g + j
                            dve.scalar_tensor_tensor(res[:, t, toks], ps[:, bank + j, 0:w],
                                                     0.5 if "down" in phase else 1.0, res[:, t, toks],
                                                     ALU.mult, ALU.add).then_inc(emptied, 1)
                    if phase == "out_cf" and at_step == 1:
                        for j in range(SET):
                            operand("gu2", phase, SET * g + j)
                            add_square("gu2", phase, SET * g + j)
                    if "down" in phase and at_step:
                        for j in (0, 1) if at_step == 1 else (2, 3):
                            operand("ag" if phase == "down1" else "down2", phase, SET * g + j)
                            add_square("ag" if phase == "down1" else "down2", phase, SET * g + j)

            def conv_adds(phase, b):
                for pair, n, q in steps_after(phase, b):
                    tiles = slice(2 * pair, 2 * pair + 2)
                    if n == 0:
                        dve.wait_ge(cf_first, 2 * (pair + 1))
                        dve.wait_ge(cf_second, 2 * (pair + 1))
                    if n < STEPS - 1:
                        dst = zd[:, :, :] if n % 2 else zc[:, tiles, :]
                        products = 2 * (q - pair) + 2
                        dve.wait_ge(cf_product, products)
                        if n >= 2:
                            dve.wait_ge(cf_step, q - 1)
                        dve.tensor_tensor(dst, dst, tap_product[:, q % PRODUCTS, :, :],
                                          ALU.add).then_inc(cf_step, 1)
                    else:
                        dve.wait_ge(cf_step, q)
                        dve.tensor_tensor(zc[:, tiles, :], zc[:, tiles, :], zd[:, :, :],
                                          ALU.add).then_inc(cf_step, 1)
                        dve.wait_ge(cf_step, q + 1)
                        for c in (2 * pair, 2 * pair + 1):
                            if c == 0:
                                dve.tensor_copy(ln_sum[:, :], zc[:, 0, :]).then_inc(ln_added, 1)
                            else:
                                dve.wait_ge(ln_added, c)
                                dve.tensor_tensor(ln_sum[:, :], ln_sum[:, :], zc[:, c, :],
                                                  ALU.add).then_inc(ln_added, 1)

            def layernorm(b):
                if b == 8:
                    dve.wait_ge(ln_mean_done, 1)
                    dve.tensor_scalar(ln_mu[:, :], ps[:, 0, SEQ:2 * SEQ], 1.0 / DS, None,
                                      ALU.mult).then_inc(ln_mu_set, 1)
                    dve.wait_ge(ln_mu_set, 1)
                    dve.tensor_tensor(zc[:, :, :], zc[:, :, :], over_two(ln_mu[:, :], SEQ, KS),
                                      ALU.subtract).then_inc(centred, 1)
                if b == 10:
                    dve.wait_ge(ln_sq, 1)
                    dve.tensor_reduce(ln_sum[:, :], y_f[:, :, :].rearrange("p c t -> p t c"),
                                      mybir.AxisListType.X, ALU.add).then_inc(ln_var_sum, 1)
                if b == 12:
                    dve.wait_ge(ln_var_done, 1)
                    dve.tensor_scalar(step[:, 0, 0:SEQ], ps[:, SET, SEQ:2 * SEQ], 1.0 / DS, EPS, ALU.mult,
                                      ALU.add).then_inc(ln_var, 1)
                if b == 13:
                    inverse_root(ln_rstd[:, :], step[:, 0, 0:SEQ], step[:, 1, 0:SEQ], ln_mu[:, :],
                                 step[:, 2, 0:SEQ], ln_sd, ln_newton)
                    dve.tensor_tensor(zc[:, :, :], zc[:, :, :], over_two(ln_rstd[:, :], SEQ, KS),
                                      ALU.mult).then_inc(normed, 1)
                if b == 15:
                    for h in range(KS // SET):
                        half = slice(SET * h, SET * (h + 1))
                        dve.wait_ge(ycf_hi, h + 1)
                        dve.tensor_tensor(y_lo[:, KS + half.start:KS + half.stop, :], y_f[:, half, :],
                                          y_hi[:, KS + half.start:KS + half.stop, :].bitcast(F32),
                                          ALU.subtract).then_inc(ycf_lo, 1)

            for q in range(4):
                for t in range(4 * q, 4 * q + 4):
                    dve.wait_ge(x_turned, t + 1)
                    bank = t if t < 8 else 4 + (t - 7) % 4
                    dve.tensor_copy(res[:, t, :], ps[:, bank, 0:T]).then_inc(emptied, 1)
                for t in range(4 * q, 4 * q + 4):
                    operand("gu1", "start", t)
                for i in (2 * q, 2 * q + 1):
                    low("gu1", 0, i)
                for t in range(4 * q, 4 * q + 4):
                    add_square("gu1", "start", t)

            parity_of = [0]

            def phase_blocks(phase, norm=None, between=None):
                def body(g, parity):
                    parity_of[0] = 1 - parity
                    for i in range(n_blocks[phase]):
                        if not (phase == "gu1" and isinstance(g, int) and g == 0):
                            low(phase, g, i)
                        if i in (2, 3, 4):
                            finish(*previous(phase, g), i - 2)
                        if norm and isinstance(g, int) and g == 0 and i == 7:
                            toks = tokens(phase)
                            dve.wait_ge(stats_done[norm], 1)
                            dve.tensor_scalar(step[:, 0, toks], ps[:, 7, 0:width[phase]], 1.0 / D, EPS,
                                              ALU.mult, ALU.add).then_inc(var_ready[norm], 1)
                        if norm and isinstance(g, int) and g == 1 and i == 0:
                            toks = tokens(phase)
                            inverse_root(rstd[:, toks], step[:, 0, toks], step[:, 1, toks], sq[:, 0, toks],
                                         step[:, 2, toks], sd_ready[norm], newton[norm])
                        if between:
                            between(n_blocks[phase] * g + i)
                return body

            def run(phase, norm=None, between=None):
                body = phase_blocks(phase, norm, between)
                n = n_groups[phase]
                if n > SET:
                    body(0, 0)
                    body(1, 1)
                    with dve.Fori(2, n, 2) as g:
                        body(g, 0)
                        body(g + 1, 1)
                else:
                    for g in range(n):
                        body(g, g % 2)

            run("gu1", "start")
            run("down1")

            def ag_between(b):
                if b == 4:
                    dve.memset(z[:, :, 0:PAD], 0.0).then_inc(pad_set, 1)
                conv_adds("ag", b)

            def out_between(b):
                conv_adds("out_sc", b)
                layernorm(b)

            run("ag", "down1", ag_between)
            run("cv", None, lambda b: conv_adds("cv", b))
            run("b", None, lambda b: conv_adds("b", b))
            run("out_sc", None, out_between)
            run("out_cf")
            run("gu2", "out_cf")

            def turned_output(b):
                g, i = divmod(b, n_blocks["down2"])
                if g >= 1 and i == 10:
                    dve.wait_ge(o_turned, g)
                    bank = SET * ((g - 1) % 2) + 2
                    dve.tensor_copy(o_tok[:, 1, (g - 1) * 512:g * 512].rearrange("p (j n) -> p j n", n=2 * P),
                                    ps[:, bank:bank + 2, SEQ:2 * SEQ]).then_inc(o_copied_v, 1)
            run("down2", None, turned_output)
            for s in range(3):
                finish("down2", G_D - 1, s)
            dve.wait_ge(stats_done["down2"], 1)
            dve.tensor_scalar(tok[:, 0, :], ps[:, 0, 0:HALVES], 1.0 / D, EPS, ALU.mult,
                              ALU.add).then_inc(var_ready["down2"], 1)
            inverse_root(tok[:, 3, :], tok[:, 0, :], tok[:, 1, :], tok[:, 2, :], tok[:, 3, :],
                         sd_ready["down2"], newton["down2"])
            dve.wait_ge(o_copied_v, G_D - 1)
            for cols in out_pieces:
                if cols.stop < D:
                    dve.tensor_scalar(o_tok[:, 1, cols], o_tok[:, 1, cols], tok[:, 3, 1:2], None,
                                      ALU.mult).then_inc(o_scaled_v, 1)
            dve.wait_ge(o_turned, G_D)
            dve.tensor_scalar(o_tok[:, 1, cols].rearrange("p (j n) -> p j n", n=2 * P),
                              ps[:, SET + 2:SET + 4, SEQ:2 * SEQ], tok[:, 3, 1:2], None,
                              ALU.mult).then_inc(o_scaled_v, 1)


_INS = ["x", "meta_tokens", "ffn1_norm", "ffn1_w_gate", "ffn1_w_up", "ffn1_w_down", "mix_norm", "w_in",
        "b_in", "conv_sc_w", "conv_cf_w", "conv_cf_b", "ln_cf_g", "ln_cf_b", "w_out",
        "ffn2_norm", "ffn2_w_gate", "ffn2_w_up", "ffn2_w_down", "final_norm"]


def kernel(**inputs):
    import numpy as np
    import concourse.bacc as bacc
    from concourse.bass_utils import run_bass_kernel_spmd

    nc = bacc.Bacc("TRN2", target_bir_lowering=False, num_devices=1)
    arrays, args = {}, []
    for name in _INS:
        a = np.ascontiguousarray(inputs[name])
        arrays[f"in_{name}"] = a
        args.append(nc.dram_tensor(f"in_{name}", a.shape, mybir.dt.from_np(a.dtype), kind="ExternalInput").ap())
    out = nc.dram_tensor("out_y", inputs["x"].shape, F32, kind="ExternalOutput").ap()
    build(nc, *args, out)
    return run_bass_kernel_spmd(nc, [arrays], core_ids=[0]).results[0]["out_y"]
```

```python
from contextlib import ExitStack

import concourse.bass as bass
from concourse import mybir

ALU = mybir.AluOpType
ACT = mybir.ActivationFunctionType
F32 = mybir.dt.float32
F32R = mybir.dt.float32r

P = 128
EPS = 1e-6
BLOCK = 1024
RING = 4
BANK = 512
SET = 4


def build(nc, x, meta_tokens, ffn1_norm, ffn1_w_gate, ffn1_w_up, ffn1_w_down, mix_norm, w_in, b_in,
          conv_sc_w, conv_cf_w, conv_cf_b, ln_cf_g, ln_cf_b, w_out,
          ffn2_norm, ffn2_w_gate, ffn2_w_up, ffn2_w_down, final_norm, out):
    D = x.shape[2]
    SEQ = x.shape[1]
    META = meta_tokens.shape[0]
    T = META + SEQ
    FF = ffn1_w_gate.shape[2]
    KD = D // P
    KF = FF // P
    DS = conv_sc_w.shape[2]
    KS = DS // P
    SCW = conv_sc_w.shape[1]
    CFW = conv_cf_w.shape[1]
    PAD = CFW - 1 - META
    HALVES = SEQ // P
    ALL = slice(0, T)
    KEPT = slice(META, T)

    G_FF = KF // 2
    G_D = KD // SET
    G_MIX = KS // 2
    G_B = KS // SET
    N_GU = 2 * KD // 4
    N_DOWN = KF // 2
    N_B = KD // 2
    N_OUT = KS // 2

    sizes = [("gu1", G_FF, N_GU), ("down1", G_D, N_DOWN), ("ag", G_MIX, N_GU), ("cv", G_MIX, N_GU),
             ("b", G_B, N_B), ("out_sc", G_D, N_OUT), ("out_cf", G_D, N_OUT),
             ("gu2", G_FF, N_GU), ("down2", G_D, N_DOWN)]
    block0, group0, n_groups, n_blocks = {}, {}, {}, {}
    blocks = groups = 0
    for name, n_g, n_b in sizes:
        block0[name], group0[name], n_groups[name], n_blocks[name] = blocks, groups, n_g, n_b
        blocks += n_g * n_b
        groups += n_g
        assert n_g % 2 == 0 and blocks % RING == 0
    before = {b[0]: a[0] for a, b in zip(sizes, sizes[1:])}

    with ExitStack() as ctx:
        def sb(name, shape, dt=F32):
            return ctx.enter_context(nc.sbuf_tensor(name, shape, dt))

        def sem(name):
            return ctx.enter_context(nc.semaphore(name))

        ps = ctx.enter_context(nc.psum_tensor("ps", [P, 2 * SET, BANK], F32))

        sb("x_region", [P, 2 * KD * T])
        x_at = nc.sbuf_base - 4 * 2 * KD * T
        sb("a_region", [P, 2 * KF * T])
        a_at = nc.sbuf_base - 4 * 2 * KF * T

        raw = [sb(f"raw{i}", [P, BLOCK]) for i in range(RING)]
        w_hi = [sb(f"w_hi{i}", [P, BLOCK], F32R) for i in range(RING)]
        w_lo = [sb(f"w_lo{i}", [P, BLOCK], F32R) for i in range(RING)]
        res = sb("res", [P, KD, T])
        t1 = sb("t1", [P, 2, T])
        t2 = sb("t2", [P, 2, T])
        rstd = sb("rstd", [P, T])
        sq_sum = sb("sq_sum", [P, T])
        sq = sb("sq", [P, 2, T])
        step = sb("step", [P, 3, T])
        par = sb("par", [P, 4, P])
        gain1 = sb("gain1", [P, KD])
        ident = sb("ident", [P, P])
        ones = sb("ones", [P, P])
        ident2 = sb("ident2", [P, P])
        tok = sb("tok", [P, 4, HALVES])
        tok_sums = sb("tok_sums", [P, HALVES, G_D])

        def at(name, offset, shape, dt=F32):
            return nc.alloc_sbuf_tensor_at(name, shape, dt, offset=offset)

        x_hi = at("x_hi", x_at, [P, KD, T], F32R)
        x_lo = at("x_lo", x_at + 4 * KD * T, [P, KD, T], F32R)
        o_tok = at("o_tok", x_at, [P, HALVES, D])
        gain_tok = at("gain_tok", x_at + 4 * HALVES * D, [P, D])
        sq_tok = at("sq_tok", x_at + 4 * (HALVES + 1) * D, [P, HALVES, BANK])
        a_hi = at("a_hi", a_at, [P, KF, T], F32R)
        a_lo = at("a_lo", a_at + 4 * KF * T, [P, KF, T], F32R)
        x_tok = at("x_tok", a_at, [P, HALVES, D])
        m_tok = at("m_tok", a_at + 4 * HALVES * D, [P, D])
        par_rows = at("par_rows", a_at + 4 * (HALVES + 1) * D, [P, 4, P])
        gain_rows = at("gain_rows", a_at + 4 * (HALVES + 1) * D + 16 * P, [KD, P])
        tile_bytes = 4 * SEQ
        y_hi = at("y_hi", a_at, [P, 2 * KS, SEQ], F32R)
        y_lo = at("y_lo", a_at + 2 * KS * tile_bytes, [P, 2 * KS, SEQ], F32R)
        y_f = at("y_f", a_at + 4 * KS * tile_bytes, [P, KS, SEQ])
        cs = at("cs", a_at + 5 * KS * tile_bytes, [P, KS, SEQ])
        zc = at("zc", a_at + 6 * KS * tile_bytes, [P, KS, SEQ])
        z = at("z", a_at + 7 * KS * tile_bytes, [P, KS, PAD + T])
        ln_at = a_at + 7 * KS * tile_bytes + 4 * KS * (PAD + T)
        ln_sum = at("ln_sum", ln_at, [P, SEQ])
        ln_mu = at("ln_mu", ln_at + tile_bytes, [P, SEQ])
        ln_rstd = at("ln_rstd", ln_at + 2 * tile_bytes, [P, SEQ])
        zd = at("zd", ln_at + 3 * tile_bytes, [P, 2, SEQ])
        PRODUCTS = 6
        tap_product = at("tap_product", ln_at + 5 * tile_bytes, [P, PRODUCTS, 2, SEQ])
        assert ln_at + (5 + 2 * PRODUCTS) * tile_bytes <= a_at + 4 * 2 * KF * T

        rows0 = [("mix", mix_norm[0], KD), ("ffn2", ffn2_norm[0], KD),
                 ("cf_b", conv_cf_b[0], KS), ("ln_g", ln_cf_g[0], KS),
                 ("ln_b", ln_cf_b[0], KS)]
        row0, used = {}, 0
        for name, _, n in rows0:
            row0[name] = used
            used += n
        row0["sc_w"] = used
        n_rows = [used + SCW * KS, b_in.shape[1] // P, P, CFW * KS - P]

        def param(name, i):
            if name == "ffn1":
                return gain1[:, i:i + 1]
            return par[:, 0, row0[name] + i:row0[name] + i + 1]

        def bias_in(i):
            return par[:, 1, i:i + 1]

        def cf_tap(k, c):
            row = k * KS + c
            return par[:, 2 + row // P, row % P:row % P + 1]

        raw_loaded = [sem(f"raw_loaded{i}") for i in range(RING)]
        hi_ready = sem("hi_ready")
        lo_ready = sem("lo_ready")
        block_used = sem("block_used")
        emptied = sem("emptied")
        gain_loaded, gain_turned, gain_ready = sem("gain_loaded"), sem("gain_turned"), sem("gain_ready")
        par_loaded, x_loaded = sem("par_loaded"), [sem(f"x_loaded{i}") for i in range(5)]
        ones_set, ident_zero, ident_set = sem("ones_set"), sem("ident_zero"), sem("ident_set")
        par_turned, par_ready, x_turned = sem("par_turned"), sem("par_ready"), sem("x_turned")
        gain_of = {"start": "ffn1", "down1": "mix", "out_cf": "ffn2"}
        xhi_ready, xlo_ready, sq_ready, sum_ready, stats_done, var_ready, sd_ready, newton = (
            {n: sem(f"{what}_{n}") for n in gain_of}
            for what in ("xhi_ready", "xlo_ready", "sq_ready", "sum_ready", "stats_done", "var_ready",
                         "sd_ready", "newton"))
        silu_ready, prod_ready, ahi_ready, alo_ready = (
            {n: sem(f"{what}_{n}") for n in ("gu1", "gu2")}
            for what in ("silu_ready", "prod_ready", "ahi_ready", "alo_ready"))
        pad_set, sig_ready, z_ready = sem("pad_set"), sem("sig_ready"), sem("z_ready")
        c_ready, cv_ready, sc_step = sem("c_ready"), sem("cv_ready"), sem("sc_step")
        cf_step, ln_added = sem("cf_step"), sem("ln_added")
        cf_first, cf_second, cf_product = sem("cf_first"), sem("cf_second"), sem("cf_product")
        sc_first = sem("sc_first")
        gain_spread, tile_done = sem("gain_spread"), sem("tile_done")
        sums_set, tok_read = sem("sums_set"), sem("tok_read")
        last_var_sum, last_var = sem("last_var_sum"), sem("last_var")
        last_sd, last_newton = sem("last_sd"), sem("last_newton")
        ysc_ready, ysc_hi, ysc_lo = sem("ysc_ready"), sem("ysc_hi"), sem("ysc_lo")
        ln_mean_done, ln_mu_set, centred = sem("ln_mean_done"), sem("ln_mu_set"), sem("centred")
        ln_sq, ln_var_sum, ln_var_done = sem("ln_sq"), sem("ln_var_sum"), sem("ln_var_done")
        ln_var, ln_sd, ln_newton, normed = sem("ln_var"), sem("ln_sd"), sem("ln_newton"), sem("normed")
        ycf_ready, ycf_hi, ycf_lo = sem("ycf_ready"), sem("ycf_hi"), sem("ycf_lo")
        o_scaled_s, o_scaled_v, stored = sem("o_scaled_s"), sem("o_scaled_v"), sem("stored")

        def before_block(phase, g, i):
            return block0[phase] + i + n_blocks[phase] * g

        def slot(phase, g, i):
            return (n_blocks[phase] * g + i) % RING if isinstance(g, int) else i % RING

        def turn(phase, g, i):
            if isinstance(g, int):
                return (block0[phase] + n_blocks[phase] * g + i) // RING
            return (block0[phase] + i) // RING + n_blocks[phase] // RING * g

        def banks_before(phase, g):
            return KD + SET * group0[phase] + SET * g

        def previous(phase, g):
            if not isinstance(g, int) or g > 0:
                return phase, g - 1
            return (before[phase], n_groups[before[phase]] - 1) if phase in before else ("", 0)

        def over_all_but_two(engine, phase, body):
            n = n_groups[phase]
            body(0, 0)
            body(1, 1)
            if n > SET:
                with engine.Fori(2, n, 2) as g:
                    body(g, 0)
                    body(g + 1, 1)
            else:
                for g in range(2, n):
                    body(g, g % 2)

        def over_groups(engine, phase, body):
            n = n_groups[phase]
            body(0, 0)
            if n > SET:
                with engine.Fori(1, n - 1, 2) as g:
                    body(g, 1)
                    body(g + 1, 0)
            else:
                for g in range(1, n - 1):
                    body(g, g % 2)
            if n > 1:
                body(n - 1, 1)

        NEAR = SEQ + -(-(SCW - 1) // 4) * 4
        width = {"gu1": T, "down1": T, "ag": T, "cv": NEAR, "b": SEQ, "out_sc": SEQ, "out_cf": SEQ,
                 "gu2": SEQ, "down2": SEQ}

        def tokens(phase):
            return slice(T - width[phase], T)

        STEPS = CFW - 1
        spread = {"ag": [0] * (N_GU + 5) + [2, 3, 2] + [2, 2, 2, 1, 2, 2, 3, 2] * (G_MIX - 2),
                  "cv": [2, 2, 1, 1, 0, 2, 2, 2] * G_MIX,
                  "b": [2, 2, 0, 1, 1, 2, 2, 2] * G_B,
                  "out_sc": [0, 0, 0, 3, 4, 2]}
        first_step, steps_left = {}, STEPS * KS // 2
        for name in spread:
            first_step[name] = STEPS * KS // 2 - steps_left
            steps_left = max(0, steps_left - sum(spread[name]))
        assert steps_left == 0

        def steps_after(phase, b):
            if phase not in spread or b >= len(spread[phase]):
                return []
            q = first_step[phase] + sum(spread[phase][:b])
            return [(*divmod(i, STEPS), i) for i in range(q, min(q + spread[phase][b], STEPS * KS // 2))]

        out_pieces = [slice(g * BANK, (g + 1) * BANK) for g in range(G_D)]

        start_squares = [buffer[:, j, :] for buffer in (sq, t1, t2) for j in range(2)]

        block = ctx.enter_context(nc.Block())

        @block.sync
        def _(sp):
            def load_x(i):
                cols = slice(i * (D // 4), (i + 1) * (D // 4))
                sp.dma_start(x_tok[:, :, cols],
                             x[0, :, cols].rearrange("(h p) d -> p h d", p=P)).then_inc(x_loaded[i], 16)

            def load(phase, g, i, src, n):
                ahead, s = before_block(phase, g, i), slot(phase, g, i)
                if not isinstance(ahead, int) or ahead >= RING:
                    sp.wait_ge(lo_ready, ahead - (RING - 1))
                sp.dma_start(raw[s][:, :].rearrange("p (c n) -> p c n", n=n), src).then_inc(raw_loaded[s], 16)

            def paired(phase, wa, wb, col_a, col_b):
                rows = [w.rearrange("(q c p) n -> q p c n", c=4, p=P) for w in (wa, wb)]

                def body(g, parity):
                    for i in range(n_blocks[phase]):
                        if phase == "gu1" and isinstance(g, int) and g == 0 and i < 4:
                            load_x(i)
                        src = rows[i % 2][i // 2, :, :, bass.ds(g * 256 + (col_a, col_b)[i % 2], 256)]
                        load(phase, g, i, src, 256)
                over_groups(sp, phase, body)

            def single(phase, w, first_row):
                rows = w.rearrange("(k c p) n -> k p c n", c=2, p=P)

                def body(g, parity):
                    for i in range(n_blocks[phase]):
                        load(phase, g, i, rows[first_row // (2 * P) + i, :, :, bass.ds(g * 512, 512)], 512)
                        if phase == "down2" and g == 0 and i == RING:
                            sp.wait_ge(block_used, block0["down2"])
                            sp.dma_start(gain_tok[:, :], final_norm.unsqueeze(0).broadcast_to([P, D])
                                         ).then_inc(gain_spread, 16)
                over_groups(sp, phase, body)

            paired("gu1", ffn1_w_gate[0], ffn1_w_up[0], 0, 0)
            single("down1", ffn1_w_down[0], 0)
            paired("ag", w_in[0], w_in[0], 3 * DS, 4 * DS)
            paired("cv", w_in[0], w_in[0], DS, 2 * DS)
            single("b", w_in[0], 0)
            single("out_sc", w_out[0], 0)
            single("out_cf", w_out[0], DS)
            paired("gu2", ffn2_w_gate[0], ffn2_w_up[0], 0, 0)
            single("down2", ffn2_w_down[0], 0)

            for i, cols in enumerate(out_pieces):
                sp.wait_ge(o_scaled_s, i + 1)
                sp.dma_start(out[0, 0:P, cols], o_tok[:, 0, cols]).then_inc(stored, 16)
                sp.wait_ge(o_scaled_v, i + 1)
                sp.dma_start(out[0, P:2 * P, cols], o_tok[:, 1, cols]).then_inc(stored, 16)
            sp.wait_ge(stored, 32 * len(out_pieces))

        @block.gpsimd
        def _(pool):
            pool.memset(ident[:, :], 0.0).then_inc(ident_zero, 1)
            pool.wait_ge(ident_zero, 1)
            pool.affine_select(out=ident[:, :], in_=ident[:, :], compare_op=ALU.not_equal, fill=1.0, base=0,
                               pattern=[[-1, P]], channel_multiplier=1).then_inc(ident_set, 1)
            pool.memset(ident2[:, :], 0.0).then_inc(ident_zero, 1)
            pool.wait_ge(ident_zero, 2)
            pool.affine_select(out=ident2[:, :], in_=ident2[:, :], compare_op=ALU.not_equal, fill=2.0, base=0,
                               pattern=[[-1, P]], channel_multiplier=1).then_inc(ident_set, 1)
            for name, src, n in rows0:
                pool.dma_start(par_rows[row0[name]:row0[name] + n, 0, :],
                               src.rearrange("(r p) -> r p", p=P)).then_inc(par_loaded, 16)
            pool.dma_start(par_rows[row0["sc_w"]:n_rows[0], 0, :],
                           conv_sc_w[0].rearrange("k (c p) -> (k c) p", p=P)).then_inc(par_loaded, 16)
            pool.dma_start(par_rows[0:n_rows[1], 1, :],
                           b_in[0].rearrange("(r p) -> r p", p=P)).then_inc(par_loaded, 16)
            taps = conv_cf_w[0].rearrange("k (c p) -> (k c) p", p=P)
            pool.dma_start(par_rows[0:P, 2, :], taps[0:P, :]).then_inc(par_loaded, 16)
            pool.dma_start(par_rows[0:n_rows[3], 3, :], taps[P:P + n_rows[3], :]).then_inc(par_loaded, 16)
            pool.wait_ge(sq_ready["start"], 1)
            pool.tensor_copy(sq_sum[:, :], start_squares[0]).then_inc(sum_ready["start"], 1)
            for t in range(1, KD):
                pool.wait_ge(sq_ready["start"], t + 1)
                pool.wait_ge(sum_ready["start"], t)
                pool.tensor_tensor(sq_sum[:, :], sq_sum[:, :], start_squares[t % len(start_squares)],
                                   ALU.add).then_inc(sum_ready["start"], 1)

        @block.tensor
        def _(pe):
            def turn_x(c, bank):
                cols = slice(c * P, (c + 1) * P)
                pe.transpose(ps[:, bank, 0:META], m_tok[0:META, cols], ident[0:META, 0:META])
                for h in range(HALVES):
                    m = pe.transpose(ps[:, bank, META + h * P:META + (h + 1) * P], x_tok[:, h, cols], ident[:, :])
                m.then_inc(x_turned, 1)

            def start_between(i):
                if i == 1:
                    pe.wait_ge(par_loaded, 16 * (len(rows0) + 4))
                    pe.wait_ge(emptied, 5)
                    for s in range(4):
                        pe.transpose(ps[:, 4, s * P:s * P + n_rows[s]], par_rows[0:n_rows[s], s, :],
                                     ident[0:n_rows[s], 0:n_rows[s]]).then_inc(par_turned, 1)
                    for c in (8, 9, 10, 11):
                        if c == 8:
                            pe.wait_ge(x_loaded[2], 16)
                        if c == 11:
                            pe.wait_ge(par_ready, 4)
                        else:
                            pe.wait_ge(emptied, c - 2)
                        turn_x(c, 4 + (c - 7) % 4)
                if i == 3:
                    pe.wait_ge(x_loaded[3], 16)
                    for c in (12, 13, 14, 15):
                        pe.wait_ge(emptied, c - 3)
                        turn_x(c, 4 + (c - 7) % 4)

            pe.wait_ge(ident_set, 1)
            pe.wait_ge(gain_loaded, 16)
            pe.transpose(ps[:, 7, 0:KD], gain_rows[:, :], ident[0:KD, 0:KD]).then_inc(gain_turned, 1)
            pe.wait_ge(x_loaded[4], 16)
            for c in range(8):
                if c % 4 == 0:
                    pe.wait_ge(x_loaded[c // 4], 16)
                if c == 7:
                    pe.wait_ge(gain_ready, 1)
                turn_x(c, c)

            def product(bank, n, w_high, w_low, act_high, act_low, first, last):
                dst = ps[:, bank, 0:n]
                pe.matmul(dst, w_high, act_high, start=first, stop=False)
                pe.matmul(dst, w_high, act_low, start=False, stop=False)
                return pe.matmul(dst, w_low, act_high, start=False, stop=last)

            def start_group(phase, g):
                if phase == "gu1" and isinstance(g, int) and g == 0:
                    pe.wait_ge(emptied, SET)
                else:
                    pe.wait_ge(emptied, banks_before(phase, g) - SET)

            def start_block(phase, g, i):
                pe.wait_ge(lo_ready, before_block(phase, g, i) + 1)

            def square_sums(norm, phase):
                pe.wait_ge(sum_ready[norm], KD)
                pe.matmul(ps[:, 7, 0:width[phase]], ones[:, :], sq_sum[:, tokens(phase)],
                          start=True, stop=True).then_inc(stats_done[norm], 1)

            def paired(phase, norm):
                toks = tokens(phase)

                def body(g, parity):
                    first_group = isinstance(g, int) and g == 0
                    start_group(phase, g)
                    if norm and isinstance(g, int) and g == 1:
                        pe.wait_ge(var_ready[norm], 1)
                    for i in range(n_blocks[phase]):
                        s = slot(phase, g, i)
                        start_block(phase, g, i)
                        for j in range(2):
                            for c in range(4):
                                k = 4 * (i // 2) + c
                                if norm and first_group and i % 2 == 0 and j == 0:
                                    pe.wait_ge(xlo_ready[norm], k + 1)
                                cols = slice(c * 256 + j * P, c * 256 + (j + 1) * P)
                                m = product(SET * parity + 2 * (i % 2) + j, width[phase],
                                            w_hi[s][:, cols], w_lo[s][:, cols],
                                            x_hi[:, k, toks], x_lo[:, k, toks], k == 0, k == KD - 1)
                        m.then_inc(block_used, 1)
                        if norm and first_group and i == (6 if norm == "start" else 3):
                            square_sums(norm, phase)
                        if norm == "start" and first_group:
                            start_between(i)
                over_groups(pe, phase, body)

            def single_group(phase, g, parity, high, low, first_k, toks, n_k, ready, per_block, extra=None):
                start_group(phase, g)
                for i in range(n_blocks[phase]):
                    s = slot(phase, g, i) if isinstance(g, int) else (n_blocks[phase] * parity + i) % RING
                    start_block(phase, g, i)
                    if ready is not None and isinstance(g, int) and g == 0:
                        pe.wait_ge(ready, per_block(i))
                    for j in range(SET):
                        for c in range(2):
                            k = 2 * i + c
                            cols = slice(c * 512 + j * P, c * 512 + (j + 1) * P)
                            m = product(SET * parity + j, width[phase], w_hi[s][:, cols], w_lo[s][:, cols],
                                        high[:, first_k + k, toks], low[:, first_k + k, toks],
                                        k == 0, k == n_k - 1)
                    m.then_inc(block_used, 1)
                    if extra:
                        extra(n_blocks[phase] * g + i)

            def last_group(g):
                pe.wait_ge(emptied, banks_before("gu2", G_FF - 1) if g < G_D // 2 else banks_before("down2", 0))
                for i in range(N_DOWN):
                    s = slot("down2", g, i)
                    start_block("down2", g, i)
                    if g == 0:
                        pe.wait_ge(alo_ready["gu2"], i + 1)
                    for h in range(HALVES):
                        toks = slice(h * P, (h + 1) * P)
                        dst = ps[:, HALVES * g + h, :]
                        for c in range(2):
                            k = 2 * i + c
                            w_high, w_low = (w[s][:, c * BANK:(c + 1) * BANK] for w in (w_hi, w_lo))
                            pe.matmul(dst, a_hi[:, k, toks], w_high, start=k == 0, stop=False)
                            pe.matmul(dst, a_lo[:, k, toks], w_high, start=False, stop=False)
                            m = pe.matmul(dst, a_hi[:, k, toks], w_low, start=False, stop=k == KF - 1)
                        if g == G_D - 1 and i == N_DOWN - 1 and h == 0:
                            m.then_inc(tile_done, 1)
                    m.then_inc(block_used, 1)
                    if i == N_DOWN // 2:
                        for h in range(HALVES):
                            for j in range(SET):
                                pe.matmul(ps[:, HALVES * g + h, j * P:(j + 1) * P],
                                          res[:, SET * g + j, META + h * P:META + (h + 1) * P], ident2[:, :],
                                          start=False, stop=False)

            def layernorm_sums(b):
                if b == 6:
                    pe.wait_ge(ln_added, KS)
                    pe.wait_ge(emptied, banks_before("out_sc", 1))
                    pe.matmul(ps[:, 0, SEQ:2 * SEQ], ones[:, :], ln_sum[:, :],
                              start=True, stop=True).then_inc(ln_mean_done, 1)
                if b == 10:
                    pe.wait_ge(ln_var_sum, 1)
                    pe.wait_ge(emptied, banks_before("out_sc", 2))
                    pe.matmul(ps[:, SET, SEQ:2 * SEQ], ones[:, :], ln_sum[:, :],
                              start=True, stop=True).then_inc(ln_var_done, 1)
                if b == 7:
                    pe.wait_ge(ln_mu_set, 1)
                if b == 11:
                    pe.wait_ge(ln_var, 1)

            pe.wait_ge(ones_set, 1)
            paired("gu1", "start")
            for g in range(G_D):
                single_group("down1", g, g % 2, a_hi, a_lo, 0, ALL, KF, alo_ready["gu1"], lambda i: i + 1)
            paired("ag", "down1")
            paired("cv", None)
            for g in range(G_B):
                single_group("b", g, g % 2, x_hi, x_lo, 0, tokens("b"), KD, None, None)
            for g in range(G_D):
                single_group("out_sc", g, g % 2, y_hi, y_lo, 0, slice(0, SEQ), KS,
                             ysc_lo, lambda i: i + 1, layernorm_sums)
            for g in range(G_D):
                single_group("out_cf", g, g % 2, y_hi, y_lo, KS, slice(0, SEQ), KS,
                             ycf_lo, lambda i: i // 2 + 1)
            paired("gu2", "out_cf")
            pe.wait_ge(ident_set, 2)
            for g in range(G_D):
                last_group(g)

        @block.scalar
        def _(act):
            act.dma_start(gain_rows[0:KD, :], ffn1_norm[0].rearrange("(r p) -> r p", p=P)).then_inc(gain_loaded, 16)
            act.dma_start(m_tok[0:META, :], meta_tokens).then_inc(x_loaded[4], 16)

            def high(phase, g, i):
                s = slot(phase, g, i)
                act.wait_ge(raw_loaded[s], 16 * turn(phase, g, i) + 16)
                ahead = before_block(phase, g, i)
                if not isinstance(ahead, int) or ahead >= RING:
                    act.wait_ge(block_used, ahead - (RING - 1))
                act.activation(w_hi[s][:, :], raw[s][:, :], ACT.Copy).then_inc(hi_ready, 1)

            def operand(phase, norm, t):
                toks = tokens(phase)
                act.wait_ge(emptied, t + 1 if norm == "start" else banks_before(norm, 0) + t + 1)
                dst = x_hi[:, t, toks]
                act.activation(dst, res[:, t, toks], ACT.Copy,
                               scale=param(gain_of[norm], t)).then_inc(xhi_ready[norm], 1)

            def square(phase, norm, t):
                toks = tokens(phase)
                if t >= 2:
                    act.wait_ge(sum_ready[norm], t - 1)
                act.activation(sq[:, t % 2, toks], res[:, t, toks], ACT.Square).then_inc(sq_ready[norm], 1)

            def token_squares(g, h):
                act.activation(sq_tok[:, h, :], ps[:, HALVES * g + h, :], ACT.Square, scale=0.5,
                               accum_out=tok_sums[:, h, g:g + 1]).then_inc(sums_set, 1)

            def root(norm, phase):
                act.wait_ge(var_ready[norm], 1)
                act.activation(step[:, 1, tokens(phase)], step[:, 0, tokens(phase)],
                               ACT.Sqrt).then_inc(sd_ready[norm], 1)

            def finish(now, phase, g, at_step):
                read = banks_before(phase, g) if phase else 0
                if phase in ("gu1", "gu2"):
                    w = width[phase]
                    if at_step == 0:
                        act.wait_ge(emptied, read + 2)
                        act.activation(t1[:, :, 0:w], t1[:, :, 0:w], ACT.Silu).then_inc(silu_ready[phase], 1)
                    if at_step == 1:
                        act.wait_ge(prod_ready[phase], g + 1)
                        act.activation(a_hi[:, bass.ds(2 * g, 2), 0:w], t2[:, :, 0:w],
                                       ACT.Copy).then_inc(ahi_ready[phase], 1)
                if phase == "down1" and at_step < 2:
                    for j in (0, 1) if at_step == 0 else (2, 3):
                        operand("ag", phase, SET * g + j)
                        square("ag", phase, SET * g + j)
                if phase == "down2" and at_step == 0:
                    act.wait_ge(block_used, before_block(phase, g, N_DOWN))
                    for h in range(HALVES):
                        token_squares(g, h)
                if phase == "out_cf" and at_step == 0:
                    for j in range(SET):
                        operand("gu2", phase, SET * g + j)
                        square("gu2", phase, SET * g + j)
                if phase == "ag" and at_step == 0:
                    act.wait_ge(emptied, read + 4)
                    for j in range(2):
                        act.activation(t2[:, j, :], t2[:, j, :], ACT.Sigmoid,
                                       bias=bias_in(4 * KS + 2 * g + j)).then_inc(sig_ready, 1)
                if phase == "cv" and at_step == 0:
                    act.wait_ge(emptied, read + 2)
                    for j in range(2):
                        act.activation(t1[:, j, 0:NEAR], t1[:, j, 0:NEAR], ACT.Identity,
                                       bias=bias_in(KS + 2 * g + j)).then_inc(c_ready, 1)
                if phase == "cv" and at_step == 1:
                    for c in (2 * g, 2 * g + 1):
                        act.wait_ge(cv_ready, c + 1)
                        act.activation(cs[:, c, :], t2[:, c % 2, NEAR - SEQ - SCW + 1:NEAR - SCW + 1], ACT.Copy,
                                       scale=param("sc_w", c)).then_inc(sc_first, 1)
                if phase == "ag" and at_step == 1:
                    act.wait_ge(pad_set, 1)
                    for c in (2 * g, 2 * g + 1):
                        act.wait_ge(z_ready, c + 1)
                        act.activation(zc[:, c, :], z[:, c, 0:SEQ], ACT.Identity, scale=cf_tap(0, c),
                                       bias=param("cf_b", c)).then_inc(cf_first, 1)
                if phase == "b" and at_step == 0:
                    for c in range(SET * g, SET * (g + 1), 2):
                        act.wait_ge(ysc_ready, c + 2)
                        act.activation(y_hi[:, c:c + 2, :], y_f[:, c:c + 2, :], ACT.Copy).then_inc(ysc_hi, 1)

            def conv_products(phase, b):
                for pair, n, q in steps_after(phase, b):
                    tiles = (2 * pair, 2 * pair + 1)
                    if n == 0:
                        act.wait_ge(z_ready, tiles[1] + 1)
                        if pair:
                            act.wait_ge(cf_step, STEPS * pair)
                        for c in tiles:
                            act.activation(zd[:, c % 2, :], z[:, c, 1:1 + SEQ], ACT.Copy,
                                           scale=cf_tap(1, c)).then_inc(cf_second, 1)
                    if n < STEPS - 1:
                        if q >= PRODUCTS:
                            act.wait_ge(cf_step, q - PRODUCTS + 1)
                        for c in tiles:
                            act.activation(tap_product[:, q % PRODUCTS, c % 2, :], z[:, c, 2 + n:2 + n + SEQ],
                                           ACT.Copy, scale=cf_tap(2 + n, c)).then_inc(cf_product, 1)

            def layernorm(b):
                if b == 10:
                    act.wait_ge(centred, 1)
                    act.wait_ge(ysc_lo, KS // 2)
                    act.activation(y_f[:, :, :], zc[:, :, :], ACT.Square).then_inc(ln_sq, 1)
                if b == 13:
                    act.wait_ge(ln_var, 1)
                    act.activation(step[:, 1, 0:SEQ], step[:, 0, 0:SEQ], ACT.Sqrt).then_inc(ln_sd, 1)
                if b in (15, 16):
                    half = slice(SET * (b - 15), SET * (b - 14))
                    act.wait_ge(normed, b - 14)
                    for c in range(half.start, half.stop):
                        act.activation(y_f[:, c, :], zc[:, c, :], ACT.Silu, scale=param("ln_g", c),
                                       bias=param("ln_b", c)).then_inc(ycf_ready, 1)
                    act.wait_ge(ycf_ready, half.stop)
                    act.activation(y_hi[:, KS + half.start:KS + half.stop, :], y_f[:, half, :],
                                   ACT.Copy).then_inc(ycf_hi, 1)

            act.wait_ge(gain_turned, 1)
            act.activation(gain1[:, :], ps[:, 7, 0:KD], ACT.Copy).then_inc(gain_ready, 1)
            act.wait_ge(gain_ready, 1)
            for q in range(4):
                high("gu1", 0, 2 * q)
                for t in range(4 * q, 4 * q + 4):
                    operand("gu1", "start", t)
                high("gu1", 0, 2 * q + 1)
                for t in range(4 * q, 4 * q + 4):
                    if t >= len(start_squares):
                        act.wait_ge(sum_ready["start"], t - len(start_squares) + 1)
                    act.activation(start_squares[t % len(start_squares)], res[:, t, :],
                                   ACT.Square).then_inc(sq_ready["start"], 1)
                if q == 1:
                    act.wait_ge(par_turned, 4)
                    for s in range(4):
                        act.activation(par[:, s, 0:n_rows[s]], ps[:, 4, s * P:s * P + n_rows[s]],
                                       ACT.Copy).then_inc(par_ready, 1)
            act.wait_ge(par_ready, 4)

            def phase_blocks(phase, norm=None, between=None):
                def body(g, parity):
                    for i in range(n_blocks[phase]):
                        if not (phase == "gu1" and isinstance(g, int) and g == 0):
                            high(phase, g, i)
                        if i in (3, 4, 5):
                            finish(phase, *previous(phase, g), i - 3)
                        if norm and isinstance(g, int) and g == 1 and i == 1:
                            root(norm, phase)
                        if phase in spread:
                            conv_products(phase, n_blocks[phase] * g + i)
                        if between:
                            between(n_blocks[phase] * g + i)
                over_all_but_two(act, phase, body)

            phase_blocks("gu1", "start")
            phase_blocks("down1")
            phase_blocks("ag", "down1")
            phase_blocks("cv")
            phase_blocks("b")
            phase_blocks("out_sc", None, layernorm)
            phase_blocks("out_cf", None, lambda b: layernorm(G_D * N_OUT + b))
            phase_blocks("gu2", "out_cf")
            phase_blocks("down2")
            act.activation(step[:, 1, 0:1], step[:, 0, 0:1], ACT.Sqrt)
            act.wait_ge(tile_done, 1)
            token_squares(G_D - 1, 0)
            act.wait_ge(block_used, before_block("down2", G_D, 0))
            token_squares(G_D - 1, 1)
            act.wait_ge(last_var, 1)
            act.activation(tok[:, 1, :], tok[:, 0, :], ACT.Sqrt).then_inc(last_sd, 1)
            act.wait_ge(last_newton, 5)
            for g, cols in enumerate(out_pieces):
                act.wait_ge(tok_read, HALVES * g + 1)
                act.activation(o_tok[:, 0, cols], o_tok[:, 0, cols], ACT.Copy,
                               scale=tok[:, 3, 0:1]).then_inc(o_scaled_s, 1)

        @block.vector
        def _(dve):
            dve.memset(ones[:, :], 1.0).then_inc(ones_set, 1)

            def low(phase, g, i):
                s = slot(phase, g, i)
                dve.wait_ge(hi_ready, before_block(phase, g, i) + 1)
                dve.tensor_tensor(w_lo[s][:, :], raw[s][:, :], w_hi[s][:, :].bitcast(F32),
                                  ALU.subtract).then_inc(lo_ready, 1)

            def operand(phase, norm, t):
                toks = tokens(phase)
                dve.wait_ge(xhi_ready[norm], t + 1)
                dve.scalar_tensor_tensor(x_lo[:, t, toks], res[:, t, toks], param(gain_of[norm], t),
                                         x_hi[:, t, toks].bitcast(F32), ALU.mult,
                                         ALU.subtract).then_inc(xlo_ready[norm], 1)

            def add_square(phase, norm, t):
                toks = tokens(phase)
                dve.wait_ge(sq_ready[norm], t + 1)
                if t == 0:
                    dve.tensor_copy(sq_sum[:, toks], sq[:, 0, toks]).then_inc(sum_ready[norm], 1)
                else:
                    dve.wait_ge(sum_ready[norm], t)
                    dve.tensor_tensor(sq_sum[:, toks], sq_sum[:, toks], sq[:, t % 2, toks],
                                      ALU.add).then_inc(sum_ready[norm], 1)

            def inverse_root(dst, var, sd, y, q, sd_done, steps):
                dve.wait_ge(sd_done, 1)
                dve.reciprocal(y, sd).then_inc(steps, 1)
                dve.wait_ge(steps, 1)
                dve.tensor_tensor(q, var, y, ALU.mult).then_inc(steps, 1)
                dve.wait_ge(steps, 2)
                dve.tensor_tensor(q, q, y, ALU.mult).then_inc(steps, 1)
                dve.wait_ge(steps, 3)
                dve.tensor_scalar(q, q, -0.5, 1.5, ALU.mult, ALU.add).then_inc(steps, 1)
                dve.wait_ge(steps, 4)
                dve.tensor_tensor(dst, q, y, ALU.mult).then_inc(steps, 1)
                dve.wait_ge(steps, 5)

            def over_two(row, w, n=2):
                return row.unsqueeze(1).broadcast_to([P, n, w])

            def finish(phase, g, at_step):
                if not phase:
                    return
                bank = SET * ((g if isinstance(g, int) else parity_of[0]) % 2)
                w, toks = width[phase], tokens(phase)
                read = banks_before(phase, g)
                ended = before_block(phase, g, n_blocks[phase])
                if phase in ("gu1", "gu2", "ag", "cv"):
                    if at_step == 0:
                        factor = over_two(rstd[:, toks], w)
                        dve.wait_ge(block_used, ended)
                        dve.tensor_tensor(t1[:, :, 0:w], ps[:, bank:bank + 2, 0:w], factor,
                                          ALU.mult).then_inc(emptied, 2)
                        dve.tensor_tensor(t2[:, :, 0:w], ps[:, bank + 2:bank + 4, 0:w], factor,
                                          ALU.mult).then_inc(emptied, 2)
                if phase in ("gu1", "gu2"):
                    if at_step == 1:
                        dve.wait_ge(silu_ready[phase], g + 1)
                        dve.wait_ge(emptied, read + 4)
                        dve.tensor_tensor(t2[:, :, 0:w], t1[:, :, 0:w], t2[:, :, 0:w],
                                          ALU.mult).then_inc(prod_ready[phase], 1)
                    if at_step == 2:
                        dve.wait_ge(ahi_ready[phase], g + 1)
                        pair = bass.ds(2 * g, 2)
                        dve.tensor_tensor(a_lo[:, pair, 0:w], t2[:, :, 0:w], a_hi[:, pair, 0:w].bitcast(F32),
                                          ALU.subtract).then_inc(alo_ready[phase], 1)
                if phase == "ag" and at_step == 1:
                    dve.wait_ge(emptied, read + 4)
                    for j in range(2):
                        c = 2 * g + j
                        dve.wait_ge(sig_ready, c + 1)
                        dve.scalar_tensor_tensor(z[:, c, PAD:PAD + T], t1[:, j, :], bias_in(3 * KS + c),
                                                 t2[:, j, :], ALU.add, ALU.mult).then_inc(z_ready, 1)
                if phase == "cv" and at_step == 1:
                    dve.wait_ge(emptied, read + 4)
                    for j in range(2):
                        c = 2 * g + j
                        dve.wait_ge(c_ready, c + 1)
                        dve.scalar_tensor_tensor(t2[:, j, 0:w], t2[:, j, 0:w], bias_in(2 * KS + c),
                                                 t1[:, j, 0:w], ALU.add, ALU.mult).then_inc(cv_ready, 1)
                if phase == "cv" and at_step == 2:
                    dve.wait_ge(sc_first, 2 * (g + 1))
                    for k in range(1, SCW):
                        for c in (2 * g, 2 * g + 1):
                            if k > 1:
                                dve.wait_ge(sc_step, (SCW - 1) * 2 * g + 2 * (k - 2) + c % 2 + 1)
                            off = NEAR - SEQ - SCW + 1 + k
                            dve.scalar_tensor_tensor(cs[:, c, :], t2[:, c % 2, off:off + SEQ],
                                                     param("sc_w", k * KS + c), cs[:, c, :], ALU.mult,
                                                     ALU.add).then_inc(sc_step, 1)
                if phase == "b" and at_step == 0:
                    dve.wait_ge(block_used, ended)
                    for c in range(SET * g, SET * (g + 1), 2):
                        half = bank + c % SET
                        dve.tensor_tensor(y_f[:, c:c + 2, :], ps[:, half:half + 2, 0:SEQ],
                                          over_two(rstd[:, toks], SEQ), ALU.mult).then_inc(emptied, 2)
                        dve.wait_ge(emptied, read + c % SET + 2)
                        for t in (c, c + 1):
                            dve.scalar_tensor_tensor(y_f[:, t, :], y_f[:, t, :], bias_in(t), cs[:, t, :],
                                                     ALU.add, ALU.mult).then_inc(ysc_ready, 1)
                    for c in range(SET * g, SET * (g + 1), 2):
                        dve.wait_ge(ysc_hi, c // 2 + 1)
                        dve.tensor_tensor(y_lo[:, c:c + 2, :], y_f[:, c:c + 2, :], y_hi[:, c:c + 2, :].bitcast(F32),
                                          ALU.subtract).then_inc(ysc_lo, 1)
                if phase in ("down1", "out_sc", "out_cf"):
                    if at_step == 0:
                        dve.wait_ge(block_used, ended)
                        for j in range(SET):
                            t = SET * g + j
                            dve.scalar_tensor_tensor(res[:, t, toks], ps[:, bank + j, 0:w],
                                                     0.5 if phase == "down1" else 1.0, res[:, t, toks],
                                                     ALU.mult, ALU.add).then_inc(emptied, 1)
                    if phase == "out_cf" and at_step == 1:
                        for j in range(SET):
                            operand("gu2", phase, SET * g + j)
                            add_square("gu2", phase, SET * g + j)
                    if phase == "down1" and at_step:
                        for j in (0, 1) if at_step == 1 else (2, 3):
                            operand("ag", phase, SET * g + j)
                            add_square("ag", phase, SET * g + j)
                if phase == "down2" and at_step == 2:
                    for h in range(HALVES):
                        token_gain(g, h)

            def token_gain(g, h):
                if g == 0 and h == 0:
                    dve.wait_ge(gain_spread, 16)
                dve.wait_ge(sums_set, HALVES * g + h + 1)
                cols = slice(BANK * g, BANK * (g + 1))
                dve.scalar_tensor_tensor(o_tok[:, h, cols], ps[:, HALVES * g + h, :], 0.5, gain_tok[:, cols],
                                         ALU.mult, ALU.mult).then_inc(tok_read, 1)

            def conv_adds(phase, b):
                for pair, n, q in steps_after(phase, b):
                    tiles = slice(2 * pair, 2 * pair + 2)
                    if n == 0:
                        dve.wait_ge(cf_first, 2 * (pair + 1))
                        dve.wait_ge(cf_second, 2 * (pair + 1))
                    if n < STEPS - 1:
                        dst = zd[:, :, :] if n % 2 else zc[:, tiles, :]
                        products = 2 * (q - pair) + 2
                        dve.wait_ge(cf_product, products)
                        if n >= 2:
                            dve.wait_ge(cf_step, q - 1)
                        dve.tensor_tensor(dst, dst, tap_product[:, q % PRODUCTS, :, :],
                                          ALU.add).then_inc(cf_step, 1)
                    else:
                        dve.wait_ge(cf_step, q)
                        dve.tensor_tensor(zc[:, tiles, :], zc[:, tiles, :], zd[:, :, :],
                                          ALU.add).then_inc(cf_step, 1)
                        dve.wait_ge(cf_step, q + 1)
                        for c in (2 * pair, 2 * pair + 1):
                            if c == 0:
                                dve.tensor_copy(ln_sum[:, :], zc[:, 0, :]).then_inc(ln_added, 1)
                            else:
                                dve.wait_ge(ln_added, c)
                                dve.tensor_tensor(ln_sum[:, :], ln_sum[:, :], zc[:, c, :],
                                                  ALU.add).then_inc(ln_added, 1)

            def layernorm(b):
                if b == 8:
                    dve.wait_ge(ln_mean_done, 1)
                    dve.tensor_scalar(ln_mu[:, :], ps[:, 0, SEQ:2 * SEQ], 1.0 / DS, None,
                                      ALU.mult).then_inc(ln_mu_set, 1)
                    dve.wait_ge(ln_mu_set, 1)
                    dve.tensor_tensor(zc[:, :, :], zc[:, :, :], over_two(ln_mu[:, :], SEQ, KS),
                                      ALU.subtract).then_inc(centred, 1)
                if b == 10:
                    dve.wait_ge(ln_sq, 1)
                    dve.tensor_reduce(ln_sum[:, :], y_f[:, :, :].rearrange("p c t -> p t c"),
                                      mybir.AxisListType.X, ALU.add).then_inc(ln_var_sum, 1)
                if b == 11:
                    dve.wait_ge(ln_var_done, 1)
                    dve.tensor_scalar(step[:, 0, 0:SEQ], ps[:, SET, SEQ:2 * SEQ], 1.0 / DS, EPS, ALU.mult,
                                      ALU.add).then_inc(ln_var, 1)
                if b == 13:
                    inverse_root(ln_rstd[:, :], step[:, 0, 0:SEQ], step[:, 1, 0:SEQ], ln_mu[:, :],
                                 step[:, 2, 0:SEQ], ln_sd, ln_newton)
                if b in (13, 14):
                    half = slice(SET * (b - 13), SET * (b - 12))
                    dve.tensor_tensor(zc[:, half, :], zc[:, half, :], over_two(ln_rstd[:, :], SEQ, SET),
                                      ALU.mult).then_inc(normed, 1)
                if b in (15, 16):
                    half = slice(SET * (b - 15), SET * (b - 14))
                    dve.wait_ge(ycf_hi, b - 14)
                    dve.tensor_tensor(y_lo[:, KS + half.start:KS + half.stop, :], y_f[:, half, :],
                                      y_hi[:, KS + half.start:KS + half.stop, :].bitcast(F32),
                                      ALU.subtract).then_inc(ycf_lo, 1)

            for q in range(4):
                for t in range(4 * q, 4 * q + 4):
                    dve.wait_ge(x_turned, t + 1)
                    bank = t if t < 8 else 4 + (t - 7) % 4
                    dve.tensor_copy(res[:, t, :], ps[:, bank, 0:T]).then_inc(emptied, 1)
                low("gu1", 0, 2 * q)
                for t in range(4 * q, 4 * q + 4):
                    operand("gu1", "start", t)
                low("gu1", 0, 2 * q + 1)

            parity_of = [0]

            def phase_blocks(phase, norm=None, between=None):
                def body(g, parity):
                    parity_of[0] = 1 - parity
                    for i in range(n_blocks[phase]):
                        if not (phase == "gu1" and isinstance(g, int) and g == 0):
                            low(phase, g, i)
                        if i in (2, 3, 4):
                            finish(*previous(phase, g), i - 2)
                        if norm and isinstance(g, int) and g == 0 and i == 7:
                            toks = tokens(phase)
                            dve.wait_ge(stats_done[norm], 1)
                            dve.tensor_scalar(step[:, 0, toks], ps[:, 7, 0:width[phase]], 1.0 / D, EPS,
                                              ALU.mult, ALU.add).then_inc(var_ready[norm], 1)
                        if norm and isinstance(g, int) and g == 1 and i == 1:
                            toks = tokens(phase)
                            inverse_root(rstd[:, toks], step[:, 0, toks], step[:, 1, toks], sq[:, 0, toks],
                                         step[:, 2, toks], sd_ready[norm], newton[norm])
                        if between:
                            between(n_blocks[phase] * g + i)
                return body

            def run(phase, norm=None, between=None):
                over_all_but_two(dve, phase, phase_blocks(phase, norm, between))

            run("gu1", "start")
            run("down1")

            def ag_between(b):
                if b == 4:
                    dve.memset(z[:, :, 0:PAD], 0.0).then_inc(pad_set, 1)
                conv_adds("ag", b)

            def out_between(b):
                conv_adds("out_sc", b)
                layernorm(b)

            run("ag", "down1", ag_between)
            run("cv", None, lambda b: conv_adds("cv", b))
            run("b", None, lambda b: conv_adds("b", b))
            run("out_sc", None, out_between)
            run("out_cf", None, lambda b: layernorm(G_D * N_OUT + b))
            run("gu2", "out_cf")

            run("down2")
            token_gain(G_D - 1, 0)
            dve.wait_ge(sums_set, HALVES * G_D)
            dve.tensor_reduce(tok[:, 2, :], tok_sums[:, :, :], mybir.AxisListType.X,
                              ALU.add).then_inc(last_var_sum, 1)
            dve.wait_ge(last_var_sum, 1)
            dve.tensor_scalar(tok[:, 0, :], tok[:, 2, :], 1.0 / D, EPS, ALU.mult,
                              ALU.add).then_inc(last_var, 1)
            token_gain(G_D - 1, 1)
            inverse_root(tok[:, 3, :], tok[:, 0, :], tok[:, 1, :], tok[:, 2, :], tok[:, 3, :],
                         last_sd, last_newton)
            dve.wait_ge(tok_read, HALVES * G_D)
            for cols in out_pieces:
                dve.tensor_scalar(o_tok[:, 1, cols], o_tok[:, 1, cols], tok[:, 3, 1:2], None,
                                  ALU.mult).then_inc(o_scaled_v, 1)


_INS = ["x", "meta_tokens", "ffn1_norm", "ffn1_w_gate", "ffn1_w_up", "ffn1_w_down", "mix_norm", "w_in",
        "b_in", "conv_sc_w", "conv_cf_w", "conv_cf_b", "ln_cf_g", "ln_cf_b", "w_out",
        "ffn2_norm", "ffn2_w_gate", "ffn2_w_up", "ffn2_w_down", "final_norm"]


def kernel(**inputs):
    import numpy as np
    import concourse.bacc as bacc
    from concourse.bass_utils import run_bass_kernel_spmd

    nc = bacc.Bacc("TRN2", target_bir_lowering=False, num_devices=1)
    arrays, args = {}, []
    for name in _INS:
        a = np.ascontiguousarray(inputs[name])
        arrays[f"in_{name}"] = a
        args.append(nc.dram_tensor(f"in_{name}", a.shape, mybir.dt.from_np(a.dtype), kind="ExternalInput").ap())
    out = nc.dram_tensor("out_y", inputs["x"].shape, F32, kind="ExternalOutput").ap()
    build(nc, *args, out)
    return run_bass_kernel_spmd(nc, [arrays], core_ids=[0]).results[0]["out_y"]
```
